# Optimizing a Trainium2 kernel written in Bass

```python
import math
import jax, jax.numpy as jnp
from jax import lax
import numpy as np

D_MODEL = 1024
BATCH = 1
SEQ = 256
DEPTH = 1

CHUNK = 64

D_CONV = 3 * D_MODEL // 4
CONV_WIDTH = 31
D_SSM = D_MODEL // 4
SSM_GROUP = 16
N_SSM_GROUPS = D_SSM // SSM_GROUP
SSM_STATE = 64
D_IN = 2 * D_CONV + D_SSM + 2 * D_MODEL

N_EXPERTS = 32
TOP_K = 4
D_FF_EXPERT = D_MODEL
SWIGLU_LIMIT = 7.0
SWIGLU_ALPHA = 1.702
MOE_BLOCK = 256

NORM_EPS = 1e-6

kernel_name = "hybrid_conformer_s5_moe_block"

def rms_norm(x, g):
    xf = x.astype(jnp.float32)
    y = xf * lax.rsqrt(jnp.mean(xf * xf, axis=-1, keepdims=True) + NORM_EPS)
    return (y * g.astype(jnp.float32)).astype(x.dtype)

def layer_norm(x, g, b):
    xf = x.astype(jnp.float32)
    mu = jnp.mean(xf, axis=-1, keepdims=True)
    xc = xf - mu
    y = xc * lax.rsqrt(jnp.mean(xc * xc, axis=-1, keepdims=True) + NORM_EPS)
    return (y * g.astype(jnp.float32) + b.astype(jnp.float32)).astype(x.dtype)

def conv_branch(a_val, a_gate, conv_w, conv_b, ln_g, ln_b, w_conv_out):
    v = a_val * jax.nn.sigmoid(a_gate)
    v = lax.conv_general_dilated(
        v, conv_w[:, None, :].astype(v.dtype), window_strides=(1,),
        padding=[(CONV_WIDTH - 1, 0)],
        dimension_numbers=("NWC", "WIO", "NWC"),
        feature_group_count=D_CONV) + conv_b
    v = layer_norm(v, ln_g, ln_b)
    v = jax.nn.silu(v)
    return v @ w_conv_out

def _complex_linear_combine(left, right):
    alr, ali, blr, bli = left
    arr, ari, brr, bri = right
    return (arr * alr - ari * ali,
            arr * ali + ari * alr,
            arr * blr - ari * bli + brr,
            arr * bli + ari * blr + bri)

def s5_branch(u, a_re, a_im, log_step, b_re, b_im, c_re, c_im, d_skip, w_glu, b_glu, w_ssm_out):
    bsz, seq, _ = u.shape
    f32 = jnp.float32
    ug = u.astype(f32).reshape(bsz, seq, N_SSM_GROUPS, SSM_GROUP)
    lr, li = a_re.astype(f32), a_im.astype(f32)
    dt = jnp.exp(log_step.astype(f32))[:, None]
    mag = jnp.exp(lr * dt)
    ar = mag * jnp.cos(li * dt)
    ai = mag * jnp.sin(li * dt)
    den = lr * lr + li * li
    fr = ((ar - 1.0) * lr + ai * li) / den
    fi = (ai * lr - (ar - 1.0) * li) / den
    br, bi = b_re.astype(f32), b_im.astype(f32)
    bbr = fr[..., None] * br - fi[..., None] * bi
    bbi = fr[..., None] * bi + fi[..., None] * br
    bu_r = jnp.einsum("bsgh,gph->bsgp", ug, bbr)
    bu_i = jnp.einsum("bsgh,gph->bsgp", ug, bbi)
    a_r = jnp.broadcast_to(ar[None, None], (1, seq) + ar.shape)
    a_i = jnp.broadcast_to(ai[None, None], (1, seq) + ai.shape)
    _, _, xr, xi = lax.associative_scan(_complex_linear_combine, (a_r, a_i, bu_r, bu_i), axis=1)
    y = (jnp.einsum("bsgp,ghp->bsgh", xr, c_re.astype(f32))
         - jnp.einsum("bsgp,ghp->bsgh", xi, c_im.astype(f32)))
    y = y.reshape(bsz, seq, D_SSM) + d_skip.astype(f32) * u.astype(f32)
    y = jax.nn.gelu(y).astype(u.dtype)
    y = y * jax.nn.sigmoid(y @ w_glu + b_glu)
    return y @ w_ssm_out

def hybrid_mixer(h, w_in, conv_w, conv_b, conv_ln_g, conv_ln_b, w_conv_out,
                 a_re, a_im, log_step, b_re, b_im, c_re, c_im, d_skip, w_glu, b_glu, w_ssm_out, w_out):
    proj = h @ w_in
    a_val, a_gate, u, g_conv, g_ssm = jnp.split(
        proj, [D_CONV, 2 * D_CONV, 2 * D_CONV + D_SSM, 2 * D_CONV + D_SSM + D_MODEL], axis=-1)
    y_conv = conv_branch(a_val, a_gate, conv_w, conv_b, conv_ln_g, conv_ln_b, w_conv_out)
    y_ssm = s5_branch(u, a_re, a_im, log_step, b_re, b_im, c_re, c_im, d_skip, w_glu, b_glu, w_ssm_out)
    m = jax.nn.sigmoid(g_conv) * y_conv + jax.nn.sigmoid(g_ssm) * y_ssm
    return m @ w_out

def moe(h, w_router, b_router, w_gate_up, b_gate_up, w_down, b_down):
    n_tok, d = h.shape
    logits = (h @ w_router + b_router).astype(jnp.float32)
    top_v, top_e = lax.top_k(logits, TOP_K)
    gate = jax.nn.softmax(top_v, axis=-1)
    n_assign = n_tok * TOP_K
    e_flat = top_e.reshape(n_assign).astype(jnp.int32)
    order = jnp.argsort(e_flat)
    sorted_e = e_flat[order]
    counts = jnp.zeros((N_EXPERTS,), jnp.int32).at[e_flat].add(1)
    off = jnp.cumsum(counts) - counts
    padded = (counts + MOE_BLOCK - 1) // MOE_BLOCK * MOE_BLOCK
    pend = jnp.cumsum(padded)
    poff = pend - padded
    dest_sorted = poff[sorted_e] + jnp.arange(n_assign, dtype=jnp.int32) - off[sorted_e]
    dest = jnp.zeros((n_assign,), jnp.int32).at[order].set(dest_sorted)
    n_blocks = -(-n_assign // MOE_BLOCK) + N_EXPERTS
    n_rows = n_blocks * MOE_BLOCK
    row_tok = jnp.full((n_rows,), n_tok, jnp.int32).at[dest].set(
        jnp.arange(n_assign, dtype=jnp.int32) // TOP_K)
    h_pad = jnp.concatenate([h, jnp.zeros((1, d), h.dtype)], axis=0)
    xs = h_pad[row_tok].reshape(n_blocks, MOE_BLOCK, d)
    blk_e = jnp.minimum(
        jnp.searchsorted(pend, jnp.arange(n_blocks, dtype=jnp.int32) * MOE_BLOCK, side="right"),
        N_EXPERTS - 1)

    def expert_block(args):
        xb, e = args
        gu = xb @ w_gate_up[e] + b_gate_up[e]
        g, lin = gu[:, :D_FF_EXPERT], gu[:, D_FF_EXPERT:]
        g = jnp.minimum(g, SWIGLU_LIMIT)
        lin = jnp.clip(lin, -SWIGLU_LIMIT, SWIGLU_LIMIT)
        act = g * jax.nn.sigmoid(SWIGLU_ALPHA * g) * (lin + 1.0)
        return act @ w_down[e] + b_down[e]

    ys = lax.map(expert_block, (xs, blk_e)).reshape(n_rows, d)
    return jnp.einsum("tkd,tk->td", ys[dest].reshape(n_tok, TOP_K, d), gate.astype(ys.dtype))

def setup_inputs(seed: int = 0) -> dict:
    key = jax.random.key(seed)
    ks = jax.random.split(key, 32)
    f32 = jnp.float32
    L, D, G, P, H = DEPTH, D_MODEL, N_SSM_GROUPS, SSM_STATE, SSM_GROUP
    E, F = N_EXPERTS, D_FF_EXPERT

    def nrm(k, shape, scale):
        return jax.random.normal(k, shape, f32) * scale

    log_step = jax.random.uniform(ks[9], (L, G), f32, math.log(1e-3), math.log(1e-1))
    a_re = -0.5 + nrm(ks[7], (L, G, P), 0.01)
    a_im = math.pi * jnp.arange(P, dtype=f32)[None, None, :] + nrm(ks[8], (L, G, P), 0.01)
    return {
        "x": nrm(ks[0], (BATCH, SEQ, D), 1.0),
        "norm_mix_g": 1.0 + nrm(ks[1], (L, D), 0.05),
        "w_in": nrm(ks[2], (L, D, D_IN), D ** -0.5),
        "conv_w": nrm(ks[3], (L, CONV_WIDTH, D_CONV), CONV_WIDTH ** -0.5),
        "conv_b": nrm(ks[4], (L, D_CONV), 0.02),
        "conv_ln_g": 1.0 + nrm(ks[5], (L, D_CONV), 0.05),
        "conv_ln_b": nrm(ks[6], (L, D_CONV), 0.02),
        "w_conv_out": nrm(ks[10], (L, D_CONV, D), D_CONV ** -0.5),
        "ssm_a_re": a_re,
        "ssm_a_im": a_im,
        "ssm_log_step": log_step,
        "ssm_b_re": nrm(ks[11], (L, G, P, H), (2 * H) ** -0.5),
        "ssm_b_im": nrm(ks[12], (L, G, P, H), (2 * H) ** -0.5),
        "ssm_c_re": nrm(ks[13], (L, G, H, P), (2 * P) ** -0.5),
        "ssm_c_im": nrm(ks[14], (L, G, H, P), (2 * P) ** -0.5),
        "ssm_d": nrm(ks[15], (L, D_SSM), 1.0),
        "w_ssm_glu": nrm(ks[16], (L, D_SSM, D_SSM), D_SSM ** -0.5),
        "b_ssm_glu": nrm(ks[17], (L, D_SSM), 0.02),
        "w_ssm_out": nrm(ks[18], (L, D_SSM, D), D_SSM ** -0.5),
        "w_out": nrm(ks[19], (L, D, D), D ** -0.5),
        "norm_ffn_g": 1.0 + nrm(ks[20], (L, D), 0.05),
        "w_router": nrm(ks[21], (L, D, E), D ** -0.5),
        "b_router": nrm(ks[22], (L, E), 0.01),
        "w_gate_up": nrm(ks[23], (L, E, D, 2 * F), D ** -0.5),
        "b_gate_up": nrm(ks[24], (L, E, 2 * F), 0.02),
        "w_down": nrm(ks[25], (L, E, F, D), F ** -0.5),
        "b_down": nrm(ks[26], (L, E, D), 0.02),
        "norm_final_g": 1.0 + nrm(ks[27], (D,), 0.05),
    }

def reference(x, norm_mix_g, w_in, conv_w, conv_b, conv_ln_g, conv_ln_b, w_conv_out,
              ssm_a_re, ssm_a_im, ssm_log_step, ssm_b_re, ssm_b_im, ssm_c_re, ssm_c_im, ssm_d,
              w_ssm_glu, b_ssm_glu, w_ssm_out, w_out, norm_ffn_g, w_router, b_router,
              w_gate_up, b_gate_up, w_down, b_down, norm_final_g):
    bsz, seq, d = x.shape
    for l in range(DEPTH):
        h = rms_norm(x, norm_mix_g[l])
        x = x + hybrid_mixer(h, w_in[l], conv_w[l], conv_b[l], conv_ln_g[l], conv_ln_b[l], w_conv_out[l],
                             ssm_a_re[l], ssm_a_im[l], ssm_log_step[l], ssm_b_re[l], ssm_b_im[l],
                             ssm_c_re[l], ssm_c_im[l], ssm_d[l], w_ssm_glu[l], b_ssm_glu[l],
                             w_ssm_out[l], w_out[l])
        h = rms_norm(x, norm_ffn_g[l]).reshape(bsz * seq, d)
        x = x + moe(h, w_router[l], b_router[l], w_gate_up[l], b_gate_up[l],
                    w_down[l], b_down[l]).reshape(bsz, seq, d)
    return rms_norm(x, norm_final_g)


_drawn_inputs = setup_inputs


def setup_inputs(seed=0):
    import zlib

    import numpy as np

    out = dict(_drawn_inputs(seed))
    spreads = {}
    factors = {'conv_ln_b': 2.916,
     'ssm_a_re': 64.0,
     'b_ssm_glu': 7.726,
     'b_gate_up': 5.38,
     'b_down': 6.171,
     'ssm_a_im': 2.75,
     'ssm_b_re': 4.07,
     'ssm_b_im': 5.884,
     'ssm_c_re': 3.614,
     'ssm_c_im': 3.244}
    for name, (base, spread) in spreads.items():
        noise = np.random.default_rng([zlib.crc32(name.encode()), seed]).standard_normal(out[name].shape)
        drawn = base * np.exp(spread * noise) if base else spread * noise
        out[name] = __import__('jax').numpy.asarray(drawn.astype(out[name].dtype))
    for name, factor in factors.items():
        out[name] = (out[name] * factor).astype(out[name].dtype)
    return out
```

```python
import numpy as np
import concourse.bass as bass
from concourse import mybir
from contextlib import ExitStack

F32 = mybir.dt.float32
BF16 = mybir.dt.bfloat16
I32 = mybir.dt.int32
U32 = mybir.dt.uint32
ALU = mybir.AluOpType
ACT = mybir.ActivationFunctionType
AX = mybir.AxisListType

D = 1024
T = 256
TT = T // 128
KD = D // 128
DC = 768
KC = DC // 128
W = 31
DS = 256
G, P, H = 16, 64, 16
ST = G * P // 128
E = 32
TOPK = 4
FF = 1024
CAP = 64
MORE = T // CAP - 1
EPS = 1e-6
CH = 2048
SLOTS = 24
PER = 12
NCH = 15
WRING = 6
ORDER = [3, 0, 4, 1, 6, 5, 2] + list(range(7, 15))
TWO_PI = 6.283185307179586
C1 = 6.28125
C2 = float(np.float32(np.round((TWO_PI - C1) * 2 ** 20) / 2 ** 20))
C3 = float(TWO_PI - C1 - C2)
ROUND = 12582912.0
LEVELS = 8
BLOCK_STEPS = 15
AGAIN_STEPS = 6
MORE_STEPS = MORE * BLOCK_STEPS + AGAIN_STEPS


def build(nc, x, norm_mix_g, w_in, conv_w, conv_b, conv_ln_g, conv_ln_b, w_conv_out,
          ssm_a_re, ssm_a_im, ssm_log_step, ssm_b_re, ssm_b_im, ssm_c_re, ssm_c_im, ssm_d,
          w_ssm_glu, b_ssm_glu, w_ssm_out, w_out, norm_ffn_g, w_router, b_router,
          w_gate_up, b_gate_up, w_down, b_down, norm_final_g, out):
    with ExitStack() as ctx:
        def sb(name, shape, dt=F32):
            return ctx.enter_context(nc.sbuf_tensor(name, shape, dt))

        def sem(name):
            return ctx.enter_context(nc.semaphore(name))

        ring = sb("ring", [128, SLOTS * CH])

        def at(slot, n, off=0):
            return ring[:, slot * CH + off:slot * CH + off + n]

        def grid(ap, *dims):
            names = "abcd"[:len(dims)]
            sizes = {c: d for c, d in zip(names[1:], dims[1:])}
            return ap.rearrange(f"p ({' '.join(names)}) -> p {' '.join(names)}", **sizes)

        wconv = grid(at(6, 3 * CH), KC, D)
        wssm = grid(at(12, CH), 2, D)
        wout = grid(at(13, 4 * CH), KD, D)
        wglu = grid(at(22, 512, 1536), 2, DS)
        cosT, sinT = grid(at(9, CH), ST, T), grid(at(10, CH), ST, T)
        braw = grid(at(11, CH), 2, ST, 128)
        bu = [grid(at(11, 512, 512 * i), 2, T) for i in range(2)]
        wz = [grid(at(11, 512, 1024 + 512 * i), 2, T) for i in range(2)]
        ygelu, yglu = grid(at(11, 512), 2, T), grid(at(11, 512, 512), 2, T)
        xr = grid(at(17, CH), TT, D)
        gateC = grid(at(17, CH), KD, T)
        gateS = grid(at(18, CH), KD, T)
        tab_tmp = at(18, 1024), at(18, 1024, 1024)
        bias32 = ring[0:96, 16 * CH:17 * CH]
        bT = grid(at(19, CH), ST, 2, 128)
        cT = grid(at(20, CH), ST, 2, 128)
        PADT = T + W - 1
        vT = grid(at(21, KC * PADT), KC, PADT)
        silu = grid(at(21, KC * T), KC, T)
        conv = grid(at(22, KC * T), KC, T)
        craw = grid(at(23, CH), 2, ST, 128)
        q_dve = grid(at(23, 512), 2, T)
        zz = grid(at(23, 512, 512), 2, T)
        xs = [grid(at(23, 512, 1024 + 512 * i), 2, T) for i in range(2)]
        h2T = grid(at(18, CH), TT, KD, 128)
        gffn = at(19, D)
        lg = grid(at(19, 64, 1280), TT, E)
        sel = grid(at(19, 256, 1344), TT * TOPK, E)
        mask = grid(at(19, 64, 1600), TT, E)
        v8 = grid(at(19, 16, 1664), TT, 8)
        idx8 = grid(at(19, 16, 1680), TT, 8).bitcast(U32)
        idxf = grid(at(19, 16, 1696), TT, 8)
        pe4 = grid(at(19, 8, 1712), TT, TOPK)
        gmT = ring[0:E, 19 * CH + 1728:19 * CH + 1728 + T]
        wrt = grid(at(19, KD * E, D), KD, E)
        bdown = ring[0:E, 20 * CH:20 * CH + D]
        tri, ones = at(20, 128, 1024), at(20, 128, 1152)
        rows = sb("rows", [128, TT, D])
        x_sb = rows
        area = sb("area", [128, 3584])
        hT = grid(area[:, 0:2048], KD, T)
        uT = grid(area[:, 2048:2560], 2, T)
        q_pool = grid(area[:, 2560:3072], 2, T)
        sig_a = grid(area[:, 3072:3584], 2, T)
        mean, rstdc = area[:, 3072:3328], area[:, 3328:3584]
        gc, sg, lc = area[:, 0:512], area[:, 512:1024], area[:, 1024:1536]
        actT = grid(area[:, 1536:2048], 4, 128)
        hrow, yrow = area[:, 2048:2560], area[:, 2560:3072]
        heT = grid(area[:, 3072:3584], 4, 128)
        ident = sb("ident", [128, 128])
        iota = sb("iota", [128, T], BF16)
        rank = sb("rank", [128, TT, E + 1])
        gate = sb("gate", [128, TT, E + 1])
        pick = sb("pick", [128, TT, CAP])
        spread = sb("spread", [128, TT, 2, CAP])
        spT = sb("spT", [128, 2, TT, 128])
        biasb = sb("biasb", [96, 4 * 512], BF16)
        esel = sb("esel", [96, E + 1], BF16)
        onehot = sb("onehot", [96, 2, CAP], BF16)
        nums = sb("nums", [1, 2 * E + 1], I32)
        numf = pick[0:1, :, :].rearrange("p t s -> p (t s)")[:, 0:3 * E + 1]
        late = spread[:, :, :, :].rearrange("p t d s -> p (t d s)")
        par = late[:, 0:54]
        taps = grid(late[:, 54:54 + KC * W], KC, W)
        mag = late[:, 240:248]
        par_rows = ring[0:54, 12 * CH:12 * CH + 128]
        tap_rows = at(22, DC)[0:W, :]
        ssb = grid(at(12, 256, 128), 2, ST, H)
        bbar = grid(at(12, 256, 384), 2, ST, H)
        btmp = grid(at(12, 128, 640), ST, H)
        pw = grid(at(12, LEVELS * 2 * ST, 768), LEVELS, 2, ST)
        brow = ring[0:1, 19 * CH + 1984:19 * CH + 1984 + E]
        sm = sb("sm", [128, 12])
        cld = grid(at(22, 256, 1024), 2, 2, P)
        gmask = grid(at(12, 16, 1000), 2, 8)
        hmask = at(12, 2, 1016)

        bank = [ctx.enter_context(nc.psum_tensor(f"bank{i}", [128, 512], F32)) for i in range(8)]

        p_ls, p_g, p_cb, p_lg, p_lb = par[:, 0:8], par[:, 8:16], par[:, 16:22], par[:, 22:28], par[:, 28:34]
        p_d, p_bg, p_re, p_im = par[:, 34:36], par[:, 36:38], par[:, 38:46], par[:, 46:54]
        log_steps = ring[0:ST, 12 * CH + 1018:12 * CH + 1020]
        ss, rstd, ss4 = sm[:, 0:2], sm[:, 2:4], sm[:, 4:8]
        top_sum, neg_top = sm[:, 8:10], sm[:, 10:12]
        dt8, th, lrdt, kk, rr, ra, den, t1, t2, fr, fi, pool_tmp = (at(12, ST, 900 + ST * n) for n in range(12))

        x_in = sem("x_in")
        par_in = sem("par_in")
        tap_in = sem("tap_in")
        ls_rows = sem("ls_rows")
        ssm_in = sem("ssm_in")
        c_in = sem("c_in")
        bias_in = sem("bias_in")
        glu_in = sem("glu_in")
        win_in = [sem(f"win_in{i}") for i in range(WRING)]
        wconv_in = sem("wconv_in")
        wssm_in = sem("wssm_in")
        wout_in = sem("wout_in")
        ffn_in = sem("ffn_in")
        down_in = sem("down_in")
        fin_in = sem("fin_in")
        slot_in = [sem(f"slot_in{i}") for i in range(SLOTS)]
        stored = sem("stored")
        dve_own = sem("dve_own")
        pool_own = sem("pool_own")
        act_own = sem("act_own")
        consts = sem("consts")
        params_pe = sem("params_pe")
        params_sb = sem("params_sb")
        x_sq = sem("x_sq")
        var_x = sem("var_x")
        std_x = sem("std_x")
        xr_ready = sem("xr_ready")
        xT_pe = sem("xT_pe")
        hT_ready = sem("hT_ready")
        act_dt = sem("act_dt")
        dve_th = sem("dve_th")
        act_mag = sem("act_mag")
        dve_rr = sem("dve_rr")
        act_sin = sem("act_sin")
        dve_f = sem("dve_f")
        tables = sem("tables")
        raw_ready = sem("raw_ready")
        rawT_pe = sem("rawT_pe")
        rawT_sb = sem("rawT_sb")
        win_pe = sem("win_pe")
        win_act = sem("win_act")
        win_dve = sem("win_dve")
        bu_pe = sem("bu_pe")
        bu_sb = sem("bu_sb")
        turned = sem("turned")
        scanned = sem("scanned")
        states = sem("states")
        y_pe = sem("y_pe")
        y_pre = sem("y_pre")
        y_gelu = sem("y_gelu")
        glu_pe = sem("glu_pe")
        glu_sig = sem("glu_sig")
        y_glu = sem("y_glu")
        conv_done = sem("conv_done")
        mean_pe = sem("mean_pe")
        centred = sem("centred")
        conv_sq = sem("conv_sq")
        var_pe = sem("var_pe")
        var_c = sem("var_c")
        std_c = sem("std_c")
        scaled = sem("scaled")
        silu_ready = sem("silu_ready")
        ssm_pe = sem("ssm_pe")
        ssm_gated = sem("ssm_gated")
        conv_pe = sem("conv_pe")
        mixed = sem("mixed")
        x1_pe = sem("x1_pe")
        wout_used = sem("wout_used")
        x1_sq = sem("x1_sq")
        var_h = sem("var_h")
        std_h = sem("std_h")
        h_ready = sem("h_ready")
        h2T_pe = sem("h2T_pe")
        h2T_act = sem("h2T_act")
        h2T_dve = sem("h2T_dve")
        logits_pe = sem("logits_pe")
        top8 = sem("top8")
        probs = sem("probs")
        mask_ready = sem("mask_ready")
        cum_pe = sem("cum_pe")
        gates_ready = sem("gates_ready")
        gmT_pe = sem("gmT_pe")
        gmT_sb = sem("gmT_sb")
        bdown_pe = sem("bdown_pe")
        nums_ready = sem("nums_ready")
        biasb_ready = sem("biasb_ready")
        pick_ready = sem("pick_ready")
        h_pe = sem("h_pe")
        h_row = sem("h_row")
        hT_pe = sem("hT_pe")
        h_T = sem("h_T")
        chunk_used = sem("chunk_used")
        g_clip = sem("g_clip")
        g_sig = sem("g_sig")
        act_ready = sem("act_ready")
        spT_pe = sem("spT_pe")
        spT_sb = sem("spT_sb")
        aT_pe = sem("aT_pe")
        a_T = sem("a_T")
        y_row = sem("y_row")
        spread_ready = sem("spread_ready")
        lin_ready = sem("lin_ready")
        swi = sem("swi")
        passed = sem("passed")
        step = sem("step")
        x2_pe = sem("x2_pe")
        x2_sq = sem("x2_sq")
        var_f = sem("var_f")
        std_f = sem("std_f")
        o_ready = sem("o_ready")

        block = ctx.enter_context(nc.Block())

        win_v = w_in[0].rearrange("(k p) n -> p k n", p=128)
        gu_v = w_gate_up[0].rearrange("e (k p) n -> e k p n", p=128)
        dn_v = w_down[0].rearrange("e (c k p) n -> e c p k n", k=2, p=128)

        @block.sync
        def _(sp):
            sp.dma_start(x_sb[:, :, :], x[0].rearrange("(t p) n -> p t n", p=128)).then_inc(x_in, 16)

            sp.dma_start(tap_rows, conv_w[0]).then_inc(tap_in, 16)
            for ri, src in enumerate((ssm_c_re, ssm_c_im)):
                sp.dma_start(cld[:, ri, :, :], src[0].rearrange("(c g) h p -> (g h) c p", c=2)).then_inc(c_in, 16)
            for ri, src in enumerate((ssm_b_re, ssm_b_im)):
                sp.dma_start(ssb[:, ri, :, :], src[0].rearrange("(t g) p h -> (g p) t h", g=2)).then_inc(ssm_in, 16)

            sp.wait_ge(par_in, 16 * 9)

            def load_win(c):
                if c >= WRING:
                    sp.wait_ge(win_pe, c - WRING + 1)
                sp.dma_start(grid(at(c % WRING, CH), KD, 256),
                             win_v[:, :, ORDER[c] * 256:ORDER[c] * 256 + 256]).then_inc(win_in[c % WRING], 16)

            for c in range(WRING):
                load_win(c)
            sp.dma_start(wglu, w_ssm_glu[0].rearrange("(k p) n -> p k n", p=128)).then_inc(glu_in, 16)
            for c in range(WRING, 9):
                load_win(c)
            for c in range(9, NCH):
                load_win(c)
            sp.dma_start(wconv, w_conv_out[0].rearrange("(k p) n -> p k n", p=128)).then_inc(wconv_in, 16)
            sp.wait_ge(biasb_ready, 1)
            sp.dma_start(wout, w_out[0].rearrange("(k p) n -> p k n", p=128)).then_inc(wout_in, 16)

            sp.wait_ge(tables, 1)
            sp.wait_ge(dve_f, 1)
            sp.dma_start(wssm, w_ssm_out[0].rearrange("(k p) n -> p k n", p=128)).then_inc(wssm_in, 16)

            def load(e, j, half):
                if j < KD:
                    src, dst = gu_v[e, j], at(half * PER + j, CH)
                else:
                    src, dst = dn_v[e, j - KD], grid(at(half * PER + j, CH), 2, D)
                sp.dma_start(dst, src).then_inc(slot_in[half * PER + j], 16)

            sp.wait_ge(bu_pe, ST)
            sp.dma_start(gffn, norm_ffn_g.to_broadcast([128, D])).then_inc(ffn_in, 16)
            sp.dma_start(wrt, w_router[0].rearrange("(k p) n -> p k n", p=128)).then_inc(ffn_in, 16)
            sp.dma_start(brow, b_router).then_inc(ffn_in, 16)
            sp.wait_ge(y_pe, ST)
            sp.dma_start(bdown, b_down[0]).then_inc(down_in, 16)
            sp.wait_ge(states, ST)
            load(1, 11, 1)
            load(0, 9, 0)
            load(0, 10, 0)
            for j in (3, 4, 5, 0, 1, 2):
                sp.wait_ge(win_pe, NCH - WRING + (j - (NCH - WRING)) % WRING + 1)
                load(0, j, 0)
            sp.wait_ge(silu_ready, KC)
            load(1, 10, 1)
            sp.wait_ge(ssm_pe, 4)
            load(0, 11, 0)
            load(1, 0, 1)
            sp.wait_ge(conv_pe, 4)
            for j in (6, 7, 8):
                load(0, j, 0)
            load(1, 9, 1)
            for j in (1, 2, 3, 4):
                sp.wait_ge(wout_used, j)
                load(1, j, 1)
            load(1, 5, 1)
            sp.wait_ge(bdown_pe, 1)
            sp.wait_ge(pick_ready, 1)
            for j in (6, 7, 8):
                load(1, j, 1)
            sp.wait_ge(nums_ready, 1)
            any_more = sp.value_load(nums[0:1, 2 * E:2 * E + 1], min_val=0, max_val=E)
            with sp.Fori(0, E // 2 - 1) as i:
                for half in range(2):
                    e = i * 2 + half
                    with sp.If(any_more > 0):
                        over = sp.value_load(nums[0:1, bass.ds(e, 1)], min_val=0, max_val=1)
                        with sp.If(over > 0):
                            before = sp.value_load(nums[0:1, bass.ds(e + E, 1)], min_val=0, max_val=E)
                            sp.wait_ge(step, before * MORE_STEPS + MORE_STEPS)
                            sp.sem_inc(passed, 1)
                    for j in range(PER):
                        sp.wait_ge(chunk_used, e * PER + j + 1)
                        load(e + 2, j, half)
            sp.wait_ge(chunk_used, E * PER - PER)
            sp.dma_start(at(0, D), norm_final_g.unsqueeze(0).to_broadcast([128, D])).then_inc(fin_in, 16)
            for t in range(TT):
                sp.wait_ge(o_ready, t + 1)
                sp.dma_start(out[0, t * 128:t * 128 + 128, :], at(1 + t, D)).then_inc(stored, 16)
            sp.wait_ge(stored, 16 * TT)

        @block.gpsimd
        def _(pool):
            own = [0]

            def link(ins):
                own[0] += 1
                ins.then_inc(pool_own, 1)
                pool.wait_ge(pool_own, own[0])

            g = nc.gpsimd
            link(g.memset(ident[:, :], 0.0))
            g.affine_select(out=ident[:, :], in_=ident[:, :], compare_op=ALU.not_equal, fill=1.0, base=0,
                            pattern=[[-1, 128]], channel_multiplier=1).then_inc(consts, 1)
            pool.wait_ge(par_in, 16 * 9)
            g.tensor_copy(par_rows[0:ST, :].rearrange("t (g p) -> t g p", g=2),
                          log_steps.unsqueeze(2).to_broadcast([ST, 2, P])).then_inc(ls_rows, 1)
            g.memset(vT[:, :, 0:W - 1], 0.0).then_inc(consts, 1)
            link(g.memset(gmask[:, 0, :], 1.0))
            link(g.affine_select(out=gmask[:, 0, :], in_=gmask[:, 0, :], compare_op=ALU.is_ge, fill=0.0, base=0,
                                 pattern=[[-H, 8]], channel_multiplier=1))
            link(g.affine_select(out=gmask[:, 0, :], in_=gmask[:, 0, :], compare_op=ALU.is_ge, fill=0.0, base=H - 1,
                                 pattern=[[H, 8]], channel_multiplier=-1))
            link(g.tensor_scalar(gmask[:, 1, :], gmask[:, 0, :], -1.0, None, ALU.mult))
            link(g.memset(hmask, 1.0))
            link(g.affine_select(out=hmask[:, 0:1], in_=hmask[:, 0:1], compare_op=ALU.is_ge, fill=0.0, base=P - 1,
                                 pattern=[[0, 1]], channel_multiplier=-1))
            link(g.affine_select(out=hmask[:, 1:2], in_=hmask[:, 1:2], compare_op=ALU.is_ge, fill=0.0, base=-P,
                                 pattern=[[0, 1]], channel_multiplier=1))
            pool.wait_ge(c_in, 32)
            for ri in range(2):
                for ct in range(2):
                    src = cld[:, ri, ct, :].unsqueeze(1).to_broadcast([128, 8, P])
                    dst = grid(at(23, 512, ri * 1024 + ct * 512), 8, P)
                    ins = g.tensor_tensor(dst, src, gmask[:, ri, :].unsqueeze(2).to_broadcast([128, 8, P]), ALU.mult)
                    if (ri, ct) == (1, 1):
                        ins.then_inc(raw_ready, 1)
            link(g.memset(esel[:, :], 0.0))
            for s in range(3):
                link(g.affine_select(out=esel[:, :], in_=esel[:, :], compare_op=ALU.not_equal, fill=1.0,
                                     base=-E * s, pattern=[[-1, E + 1]], channel_multiplier=1))
            g.memset(esel[:, E:E + 1], 0.0).then_inc(consts, 1)
            g.iota(iota[:, :], pattern=[[1, T]], base=0, channel_multiplier=0,
                   allow_small_or_imprecise_dtypes=True).then_inc(consts, 1)
            link(g.memset(braw[:, :, :, :], 0.0))
            pool.wait_ge(dve_f, 1)
            for ri in range(2):
                for j in range(4):
                    src = bbar[:, ri, :, :].rearrange("p (c j) h -> p j c h", j=4)[:, j].unsqueeze(2)\
                        .to_broadcast([128, 2, 2, H])
                    msk = hmask.unsqueeze(1).unsqueeze(3).to_broadcast([128, 2, 2, H])
                    dst = braw[:, ri, :, :].rearrange("p (c j) (g h) -> p j c g h", j=4, h=H)[:, j, :, 2 * j:2 * j + 2]
                    ins = g.tensor_tensor(dst, src, msk, ALU.mult)
            ins.then_inc(raw_ready, 1)
            pool.wait_ge(act_sin, 2)
            link(g.memset(cosT[:, :, 0:1], 1.0))
            link(g.memset(sinT[:, :, 0:1], 0.0))
            for k in range(LEVELS):
                L = 1 << k
                pc = pw[:, k, 0, :].unsqueeze(2).to_broadcast([128, ST, L])
                ps = pw[:, k, 1, :].unsqueeze(2).to_broadcast([128, ST, L])
                lo, hi = slice(0, L), slice(L, 2 * L)
                ta, tb = (grid(t[:, 0:ST * L], ST, L) for t in tab_tmp)
                g.tensor_tensor(cosT[:, :, hi], cosT[:, :, lo], pc, ALU.mult)
                g.tensor_tensor(ta, sinT[:, :, lo], ps, ALU.mult)
                g.tensor_tensor(sinT[:, :, hi], cosT[:, :, lo], ps, ALU.mult)
                link(g.tensor_tensor(tb, sinT[:, :, lo], pc, ALU.mult))
                g.tensor_tensor(cosT[:, :, hi], cosT[:, :, hi], ta, ALU.subtract)
                last = g.tensor_tensor(sinT[:, :, hi], sinT[:, :, hi], tb, ALU.add)
                if k == LEVELS - 1:
                    last.then_inc(tables, 1)
                else:
                    link(last)
                    c0, s0, c1, s1 = pw[:, k, 0, :], pw[:, k, 1, :], pw[:, k + 1, 0, :], pw[:, k + 1, 1, :]
                    g.tensor_tensor(c1, c0, c0, ALU.mult)
                    g.tensor_tensor(pool_tmp, s0, s0, ALU.mult)
                    link(g.tensor_tensor(s1, c0, s0, ALU.mult))
                    g.tensor_tensor(c1, c1, pool_tmp, ALU.subtract)
                    link(g.tensor_tensor(s1, s1, s1, ALU.add))
            pool.wait_ge(tables, 1)
            for t in range(ST):
                pool.wait_ge(bu_sb, t + 1)
                if t >= 2:
                    pool.wait_ge(scanned, t - 1)
                b_, w_ = bu[t % 2], wz[t % 2]
                cb = cosT[:, t, :].unsqueeze(1).to_broadcast([128, 2, T])
                sb_ = sinT[:, t, :].unsqueeze(1).to_broadcast([128, 2, T])
                g.tensor_tensor(w_, b_, cb, ALU.mult)
                link(g.tensor_tensor(q_pool, b_, sb_, ALU.mult))
                g.tensor_tensor(w_[:, 0, :], w_[:, 0, :], q_pool[:, 1, :], ALU.add)
                last = g.tensor_tensor(w_[:, 1, :], w_[:, 1, :], q_pool[:, 0, :], ALU.subtract)
                last.then_inc(turned, 1)
                pool.wait_ge(turned, t + 1)
            g.memset(rank[:, :, E:E + 1], -1.0).then_inc(consts, 1)
            g.memset(gate[:, :, E:E + 1], 0.0).then_inc(consts, 1)
            g.memset(spT[:, :, :, :], 0.0).then_inc(consts, 1)
            pool.wait_ge(y_pe, ST)
            g.memset(ones, 1.0).then_inc(consts, 1)
            link(g.memset(tri, 1.0))
            g.affine_select(out=tri, in_=tri, compare_op=ALU.is_gt, fill=0.0, base=0,
                            pattern=[[1, 128]], channel_multiplier=-1).then_inc(consts, 1)

        @block.scalar
        def _(act):
            s = nc.scalar
            act.dma_start(log_steps, ssm_log_step[0].rearrange("(t g) -> t g", g=2)).then_inc(par_in, 16)
            r0 = ST
            for src, n in ((norm_mix_g, 8), (conv_b, 6), (conv_ln_g, 6), (conv_ln_b, 6), (ssm_d, 2), (b_ssm_glu, 2)):
                act.dma_start(par_rows[r0:r0 + n, :], src[0].rearrange("(k p) -> k p", p=128)).then_inc(par_in, 16)
                r0 += n
            for src in (ssm_a_re, ssm_a_im):
                act.dma_start(par_rows[r0:r0 + ST, :], src[0].rearrange("(t g) p -> t (g p)", g=2)).then_inc(par_in, 16)
                r0 += ST
            for n in range(3):
                act.dma_start(bias32[32 * n:32 * n + 32, :], b_gate_up[0]).then_inc(bias_in, 16)
            act.wait_ge(x_in, 16)
            for t in range(TT):
                s.activation(xr[:, t, :], x_sb[:, t, :], ACT.Square, accum_out=ss[:, t:t + 1]).then_inc(x_sq, 1)
            act.wait_ge(var_x, 1)
            s.activation(rstd, ss, ACT.Sqrt).then_inc(std_x, 1)
            act.wait_ge(params_pe, 1)
            s.activation(par[:, :], bank[0][:, 0:54], ACT.Copy).then_inc(params_sb, 1)
            s.activation(taps[:, :, :], bank[0][:, 64:64 + KC * W].rearrange("p (k w) -> p k w", w=W), ACT.Copy)\
                .then_inc(params_sb, 1)
            act.wait_ge(params_sb, 1)
            for k in range(KD // 2, KD):
                act.wait_ge(xT_pe, k // 2 + 1)
                s.activation(hT[:, k, :], bank[4 + k // 2][:, k % 2 * T:k % 2 * T + T], ACT.Copy, scale=p_g[:, k:k + 1]).then_inc(hT_ready, 1)
            s.activation(dt8, p_ls, ACT.Exp).then_inc(act_dt, 1)
            act.wait_ge(dve_th, 1)
            s.activation(mag, lrdt, ACT.Exp).then_inc(act_mag, 1)
            act.wait_ge(dve_rr, 1)
            s.activation(pw[:, 0, 1, :], rr, ACT.Sin).then_inc(act_sin, 1)
            s.activation(pw[:, 0, 0, :], ra, ACT.Sin).then_inc(act_sin, 1)

            def take(n):
                c = ORDER[n]
                src = bank[4 + n % 4][:, :]
                act.wait_ge(win_pe, n + 1)
                if c in (3, 4, 5):
                    if c > 3:
                        act.wait_ge(win_dve, c - 3)
                    s.activation(sig_a, grid(src, 2, T), ACT.Sigmoid).then_inc(win_act, 1)
                elif c == 6:
                    s.activation(uT, grid(src, 2, T), ACT.Copy).then_inc(win_act, 1)
                elif c < 11:
                    s.activation(gateC[:, 2 * (c - 7):2 * (c - 7) + 2, :], grid(src, 2, T), ACT.Sigmoid).then_inc(win_act, 1)
                else:
                    s.activation(gateS[:, 2 * (c - 11):2 * (c - 11) + 2, :], grid(src, 2, T), ACT.Sigmoid).then_inc(win_act, 1)

            def bu_copy(t):
                act.wait_ge(bu_pe, t + 1)
                if t >= 2:
                    act.wait_ge(turned, t - 1)
                s.activation(bu[t % 2], grid(bank[t % 2][:, :], 2, T), ACT.Copy).then_inc(bu_sb, 1)

            take(0)
            for n in range(8):
                act.wait_ge(rawT_pe, n // 4 * 4 + 4)
                dst = (cT, bT)[n // 4]
                s.activation(dst[:, 2 * (n % 4):2 * (n % 4) + 2, :, :].rearrange("p t r c -> p (t r) c"),
                             grid(bank[n % 4][:, :], 4, 128), ACT.Copy).then_inc(rawT_sb, 1)
                if n == 3:
                    take(2)
            take(4)
            take(5)
            bu_copy(0)
            bu_copy(1)
            bu_copy(2)
            take(7)
            bu_copy(3)
            take(8)
            bu_copy(4)
            bu_copy(5)
            take(9)
            bu_copy(6)
            take(10)
            bu_copy(7)
            act.wait_ge(tables, 1)
            for n in (11, 12, 13):
                take(n)
            act.wait_ge(y_pre, 1)
            s.activation(ygelu, yglu, ACT.Gelu_apprx_tanh).then_inc(y_gelu, 1)
            for k in range(KC):
                act.wait_ge(centred, k + 1)
                s.activation(silu[:, k, :], conv[:, k, :], ACT.Square).then_inc(conv_sq, 1)
            take(14)
            act.wait_ge(glu_pe, 1)
            for m in range(2):
                s.activation(uT[:, m, :], bank[2][:, m * T:m * T + T], ACT.Sigmoid, bias=p_bg[:, m:m + 1]).then_inc(glu_sig, 1)
            act.wait_ge(var_c, 1)
            s.activation(rstdc, rstdc, ACT.Sqrt).then_inc(std_c, 1)
            for k in range(KC):
                act.wait_ge(scaled, k + 1)
                s.activation(silu[:, k, :], conv[:, k, :], ACT.Silu, scale=p_lg[:, k:k + 1], bias=p_lb[:, k:k + 1])\
                    .then_inc(silu_ready, 1)
            for t in range(TT):
                act.wait_ge(*((x1_pe, 1), (wout_used, 4))[t])
                for h in range(2):
                    last = s.activation(area[:, 512 * h + 1024 * t:512 * h + 1024 * t + 512], bank[2 * t + h][:, :], ACT.Square,
                                        accum_out=ss4[:, 2 * t + h:2 * t + h + 1])
                last.then_inc(x1_sq, 1)
                act.wait_ge(var_h, t + 1)
                s.activation(rstd[:, t:t + 1], ss[:, t:t + 1], ACT.Sqrt).then_inc(std_h, 1)
            for t in range(TT):
                act.wait_ge(h2T_pe, 2 * t + 1)
                s.activation(h2T[:, t, 0:4, :], grid(bank[4 + 2 * t][:, :], 4, 128), ACT.Copy).then_inc(h2T_act, 1)
            for t in range(TT):
                act.wait_ge(top8, t + 1)
                s.activation(pe4[:, t, :], v8[:, t, 0:TOPK], ACT.Exp, bias=neg_top[:, t:t + 1],
                             accum_out=top_sum[:, t:t + 1]).then_inc(probs, 1)
            act.wait_ge(gmT_pe, 1)
            s.activation(gmT, bank[7][0:E, 0:T], ACT.Copy).then_inc(gmT_sb, 1)

            def h_row_copy():
                return s.activation(hrow, bank[6][:, :], ACT.Copy)

            def h_T_copy():
                return s.activation(heT, grid(bank[7][:, :], 4, 128), ACT.Copy)

            def a_T_copy():
                return s.activation(actT, grid(bank[7][:, :], 4, 128), ACT.Copy)

            def y_row_copy():
                return s.activation(yrow, bank[6][:, :], ACT.Copy)

            def sigmoid():
                return s.activation(sg, gc, ACT.Sigmoid, scale=1.702)

            def spread_copy():
                s.activation(spT[0:64, 0, :, :], grid(bank[6][0:64, 0:T], 2, 128), ACT.Copy)
                return s.activation(spT[64:128, 1, :, :], grid(bank[6][64:128, 0:T], 2, 128), ACT.Copy)

            act.wait_ge(h_pe, 1)
            h_row_copy().then_inc(h_row, 1)
            act.wait_ge(hT_pe, 1)
            h_T_copy().then_inc(h_T, 1)
            act.wait_ge(nums_ready, 1)
            any_more = act.value_load(nums[0:1, 2 * E:2 * E + 1], min_val=0, max_val=E)
            with act.Fori(0, E // 2) as i:
                for half in range(2):
                    e = i * 2 + half
                    act.wait_ge(g_clip, e + 1)
                    sigmoid().then_inc(g_sig, 1)
                    act.wait_ge(h_pe, e + 2)
                    h_row_copy().then_inc(h_row, 1)
                    act.wait_ge(hT_pe, e + 2)
                    h_T_copy().then_inc(h_T, 1)
                    act.wait_ge(spT_pe, e + 1)
                    spread_copy().then_inc(spT_sb, 1)
                    act.wait_ge(aT_pe, e + 1)
                    a_T_copy().then_inc(a_T, 1)
                    act.wait_ge(chunk_used, e * PER + PER)
                    y_row_copy().then_inc(y_row, 1)
                    with act.If(any_more > 0):
                        over = act.value_load(nums[0:1, bass.ds(e, 1)], min_val=0, max_val=1)
                        with act.If(over > 0):
                            before = act.value_load(nums[0:1, bass.ds(e + E, 1)], min_val=0, max_val=E)
                            with act.Fori(0, MORE) as b:
                                o = before * MORE_STEPS + b * BLOCK_STEPS
                                act.wait_ge(step, o + 3)
                                h_row_copy().then_inc(step, 1)
                                act.wait_ge(step, o + 5)
                                h_T_copy()
                                spread_copy().then_inc(step, 1)
                                act.wait_ge(step, o + 8)
                                sigmoid().then_inc(step, 1)
                                act.wait_ge(step, o + 12)
                                a_T_copy().then_inc(step, 1)
                                act.wait_ge(step, o + 14)
                                y_row_copy().then_inc(step, 1)
                            a = before * MORE_STEPS + MORE * BLOCK_STEPS
                            act.wait_ge(step, a + 3)
                            h_row_copy().then_inc(step, 1)
                            act.wait_ge(step, a + 5)
                            h_T_copy().then_inc(step, 1)
                            act.wait_ge(step, a + 6)
                            act.sem_inc(passed, 1)
            for t in range(TT):
                act.wait_ge(x2_pe, t + 1)
                for h in range(2):
                    last = s.activation(at(4, 512, 512 * (2 * t + h)), bank[2 * t + h][:, :], ACT.Square,
                                        accum_out=ss4[:, 2 * t + h:2 * t + h + 1])
                last.then_inc(x2_sq, 1)
                act.wait_ge(var_f, t + 1)
                s.activation(rstd[:, t:t + 1], ss[:, t:t + 1], ACT.Sqrt).then_inc(std_f, 1)

        @block.vector
        def _(dve):
            v = nc.vector
            own = [0]

            def link(ins):
                own[0] += 1
                ins.then_inc(dve_own, 1)
                dve.wait_ge(dve_own, own[0])

            def var_of_sum(n):
                return v.tensor_scalar(ss, ss, 1.0 / n, EPS, ALU.mult, ALU.add)

            dve.wait_ge(x_sq, TT)
            var_of_sum(D).then_inc(var_x, 1)
            dve.wait_ge(std_x, 1)
            link(v.reciprocal(rstd, rstd))
            for t in range(TT):
                v.tensor_scalar(xr[:, t, :], x_sb[:, t, :], rstd[:, t:t + 1], None, ALU.mult).then_inc(xr_ready, 1)
            dve.wait_ge(params_sb, 1)
            for k in range(KD // 2):
                dve.wait_ge(xT_pe, k // 2 + 1)
                v.tensor_scalar(hT[:, k, :], bank[4 + k // 2][:, k % 2 * T:k % 2 * T + T], p_g[:, k:k + 1], None, ALU.mult).then_inc(hT_ready, 1)
            dve.wait_ge(act_dt, 1)
            v.tensor_tensor(th, p_im, dt8, ALU.mult)
            link(v.tensor_tensor(lrdt, p_re, dt8, ALU.mult))
            link(v.tensor_scalar(kk, th, 1.0 / TWO_PI, ROUND, ALU.mult, ALU.add))
            v.tensor_scalar(kk, kk, -ROUND, None, ALU.add).then_inc(dve_th, 1)
            dve.wait_ge(dve_th, 1)
            link(v.scalar_tensor_tensor(rr, kk, -C1, th, ALU.mult, ALU.add))
            link(v.scalar_tensor_tensor(rr, kk, -C2, rr, ALU.mult, ALU.add))
            link(v.scalar_tensor_tensor(rr, kk, -C3, rr, ALU.mult, ALU.add))
            link(v.tensor_scalar(rr, rr, 3.1415925, -3.1415925, ALU.min, ALU.max))
            link(v.scalar_tensor_tensor(ra, rr, -1.0, rr, ALU.mult, ALU.max))
            v.tensor_scalar(ra, ra, -1.0, TWO_PI / 4, ALU.mult, ALU.add).then_inc(dve_rr, 1)
            v.tensor_tensor(t1, p_re, p_re, ALU.mult)
            link(v.tensor_tensor(t2, p_im, p_im, ALU.mult))
            link(v.tensor_tensor(den, t1, t2, ALU.add))
            link(v.reciprocal(den, den))
            dve.wait_ge(act_mag, 1)
            dve.wait_ge(act_sin, 2)
            v.tensor_tensor(t1, mag, pw[:, 0, 0, :], ALU.mult)
            link(v.tensor_tensor(t2, mag, pw[:, 0, 1, :], ALU.mult))
            link(v.tensor_scalar(t1, t1, -1.0, None, ALU.add))
            v.tensor_tensor(fr, t1, p_re, ALU.mult)
            v.tensor_tensor(kk, t2, p_im, ALU.mult)
            v.tensor_tensor(fi, t2, p_re, ALU.mult)
            link(v.tensor_tensor(th, t1, p_im, ALU.mult))
            v.tensor_tensor(fr, fr, kk, ALU.add)
            link(v.tensor_tensor(fi, fi, th, ALU.subtract))
            v.tensor_tensor(fr, fr, den, ALU.mult)
            link(v.tensor_tensor(fi, fi, den, ALU.mult))
            dve.wait_ge(ssm_in, 32)
            frb = fr.unsqueeze(2).to_broadcast([128, ST, H])
            fib = fi.unsqueeze(2).to_broadcast([128, ST, H])
            link(v.tensor_tensor(btmp[:, :, :], ssb[:, 1, :, :], fib, ALU.mult))
            link(v.tensor_tensor(bbar[:, 0, :, :], ssb[:, 0, :, :], frb, ALU.mult))
            link(v.tensor_tensor(bbar[:, 0, :, :], bbar[:, 0, :, :], btmp[:, :, :], ALU.subtract))
            link(v.tensor_tensor(btmp[:, :, :], ssb[:, 0, :, :], fib, ALU.mult))
            link(v.tensor_tensor(bbar[:, 1, :, :], ssb[:, 1, :, :], frb, ALU.mult))
            v.tensor_tensor(bbar[:, 1, :, :], bbar[:, 1, :, :], btmp[:, :, :], ALU.add).then_inc(dve_f, 1)
            dve.wait_ge(bias_in, 48)
            for n in range(3):
                for m in range(n):
                    r = slice(32 * n, 32 * n + 32)
                    link(v.tensor_copy(biasb[r, :], bias32[r, :]))
                    link(v.tensor_tensor(bias32[r, :], bias32[r, :], biasb[r, :], ALU.subtract))
            for n in range(3):
                r = slice(32 * n, 32 * n + 32)
                last = v.tensor_copy(biasb[r, :], bias32[r, :])
            last.then_inc(biasb_ready, 1)

            def gated(j):
                n = ORDER.index(j)
                dve.wait_ge(win_pe, n + 1)
                dve.wait_ge(win_act, (1, 2, 4)[j])
                v.tensor_tensor(vT[:, 2 * j:2 * j + 2, W - 1:PADT], sig_a, grid(bank[4 + n % 4][:, :], 2, T),
                                ALU.mult).then_inc(win_dve, 1)
                dve.wait_ge(win_dve, j + 1)

            def convolve(j):
                for w in range(W):
                    for k in (2 * j, 2 * j + 1):
                        src = vT[:, k, w:w + T]
                        if w == 0:
                            ins = v.tensor_scalar(conv[:, k, :], src, taps[:, k, 0:1], p_cb[:, k:k + 1], ALU.mult, ALU.add)
                        else:
                            dve.wait_ge(dve_own, own[0] - 1 if w < W - 1 or k == 2 * j else own[0])
                            ins = v.scalar_tensor_tensor(conv[:, k, :], src, taps[:, k, w:w + 1], conv[:, k, :],
                                                         ALU.mult, ALU.add)
                        if w == W - 1:
                            ins.then_inc(conv_done, 1)
                        else:
                            own[0] += 1
                            ins.then_inc(dve_own, 1)
                dve.wait_ge(conv_done, 2 * j + 2)

            dve.wait_ge(consts, 2)
            gated(0)
            dve.wait_ge(raw_ready, 1)
            dve.wait_ge(params_sb, 2)
            convolve(0)
            gated(1)
            convolve(1)
            gated(2)
            for t in range(ST):
                dve.wait_ge(turned, t + 1)
                if t == 0:
                    dve.wait_ge(rawT_pe, 8)
                for ri in range(2):
                    last = v.tensor_tensor_scan(zz[:, ri, :], mag[:, t:t + 1].to_broadcast([128, T]), wz[t % 2][:, ri, :],
                                                0.0, ALU.mult, ALU.add)
                last.then_inc(scanned, 1)
                dve.wait_ge(scanned, t + 1)
                if t >= 2:
                    dve.wait_ge(y_pe, t - 1)
                cb = cosT[:, t, :].unsqueeze(1).to_broadcast([128, 2, T])
                sb_ = sinT[:, t, :].unsqueeze(1).to_broadcast([128, 2, T])
                v.tensor_tensor(xs[t % 2], zz, cb, ALU.mult)
                link(v.tensor_tensor(q_dve, zz, sb_, ALU.mult))
                v.tensor_tensor(xs[t % 2][:, 0, :], xs[t % 2][:, 0, :], q_dve[:, 1, :], ALU.subtract)
                v.tensor_tensor(xs[t % 2][:, 1, :], xs[t % 2][:, 1, :], q_dve[:, 0, :], ALU.add).then_inc(states, 1)
                dve.wait_ge(states, t + 1)
            convolve(2)
            dve.wait_ge(y_pe, ST)
            dve.wait_ge(turned, ST)
            for c in range(2):
                last = v.scalar_tensor_tensor(yglu[:, c, :], uT[:, c, :], p_d[:, c:c + 1], bank[3][:, c * T:c * T + T],
                                              ALU.mult, ALU.add)
            last.then_inc(y_pre, 1)
            dve.wait_ge(mean_pe, 1)
            link(v.tensor_scalar(mean, bank[0][:, 0:T], 1.0 / DC, None, ALU.mult))
            for k in range(KC):
                v.tensor_tensor(conv[:, k, :], conv[:, k, :], mean, ALU.subtract).then_inc(centred, 1)
            dve.wait_ge(glu_sig, 2)
            v.tensor_tensor(yglu, ygelu, uT, ALU.mult).then_inc(y_glu, 1)
            dve.wait_ge(var_pe, 1)
            v.tensor_scalar(rstdc, bank[1][:, 0:T], 1.0 / DC, EPS, ALU.mult, ALU.add).then_inc(var_c, 1)
            dve.wait_ge(std_c, 1)
            link(v.reciprocal(rstdc, rstdc))
            dve.wait_ge(centred, KC)
            for k in range(KC):
                v.tensor_tensor(conv[:, k, :], conv[:, k, :], rstdc, ALU.mult).then_inc(scaled, 1)
            dve.wait_ge(win_act, 12)
            for j in range(4):
                dve.wait_ge(ssm_pe, j + 1)
                v.tensor_tensor(gateS[:, 2 * j:2 * j + 2, :], gateS[:, 2 * j:2 * j + 2, :],
                                grid(bank[(2, 3, 0, 1)[j]][:, :], 2, T), ALU.mult).then_inc(ssm_gated, 1)
            dve.wait_ge(ssm_gated, 4)
            for j in range(4):
                dve.wait_ge(conv_pe, j + 1)
                link(v.tensor_tensor(gateC[:, 2 * j:2 * j + 2, :], gateC[:, 2 * j:2 * j + 2, :],
                                     grid(bank[4 + j][:, :], 2, T), ALU.mult))
                v.tensor_tensor(gateC[:, 2 * j:2 * j + 2, :], gateC[:, 2 * j:2 * j + 2, :], gateS[:, 2 * j:2 * j + 2, :],
                                ALU.add).then_inc(mixed, 1)

            def row_var(t):
                link(v.tensor_tensor(ss[:, t:t + 1], ss4[:, 2 * t:2 * t + 1], ss4[:, 2 * t + 1:2 * t + 2], ALU.add))
                return v.tensor_scalar(ss[:, t:t + 1], ss[:, t:t + 1], 1.0 / D, EPS, ALU.mult, ALU.add)

            def normed(t, dst, g):
                link(v.reciprocal(rstd[:, t:t + 1], rstd[:, t:t + 1]))
                for h in range(2):
                    c = slice(h * 512, h * 512 + 512)
                    last = v.scalar_tensor_tensor(dst[:, c], bank[2 * t + h][:, :], rstd[:, t:t + 1], g[:, c], ALU.mult, ALU.mult)
                return last

            dve.wait_ge(ffn_in, 48)
            for t in range(TT):
                dve.wait_ge(x1_sq, t + 1)
                row_var(t).then_inc(var_h, 1)
                dve.wait_ge(std_h, t + 1)
                normed(t, rows[:, t, :], gffn).then_inc(h_ready, 1)
            for t in range(TT):
                dve.wait_ge(h2T_pe, 2 * t + 2)
                v.tensor_copy(h2T[:, t, 4:8, :], grid(bank[5 + 2 * t][:, :], 4, 128)).then_inc(h2T_dve, 1)
            for t in range(TT):
                dve.wait_ge(logits_pe, t + 1)
                link(v.tensor_copy(lg[:, t, :], bank[4 + 2 * t][:, 0:E]))
                link(v.max(out=v8[:, t, :], in_=lg[:, t, :]))
            for t in range(TT):
                v.tensor_scalar(neg_top[:, t:t + 1], v8[:, t, 0:1], -1.0, None, ALU.mult).then_inc(top8, 1)
            for t in range(TT):
                last = v.max_index(out=idx8[:, t, :], in_max=v8[:, t, :], in_values=lg[:, t, :])
            link(last)
            link(v.tensor_copy(idxf, idx8))
            selv = sel.rearrange("p (t k) e -> p t k e", t=TT)
            dve.wait_ge(consts, 4)
            for t in range(TT):
                last = v.tensor_tensor(selv[:, t], iota[:, 0:E].unsqueeze(1).to_broadcast([128, TOPK, E]),
                                       idxf[:, t, 0:TOPK].unsqueeze(2).to_broadcast([128, TOPK, E]), ALU.is_equal)
            link(last)
            for t in range(TT):
                last = v.tensor_reduce(mask[:, t, :], selv[:, t].rearrange("p k e -> p e k"), AX.X, ALU.add)
            last.then_inc(mask_ready, 1)
            dve.wait_ge(probs, TT)
            link(v.reciprocal(top_sum, top_sum))
            for t in range(TT):
                last = v.tensor_scalar(pe4[:, t, :], pe4[:, t, :], top_sum[:, t:t + 1], None, ALU.mult)
            link(last)
            dve.wait_ge(mask_ready, 1)
            for t in range(TT):
                last = v.tensor_tensor(selv[:, t], selv[:, t], pe4[:, t, :].unsqueeze(2).to_broadcast([128, TOPK, E]), ALU.mult)
            link(last)
            for t in range(TT):
                last = v.tensor_reduce(gate[:, t, 0:E], selv[:, t].rearrange("p k e -> p e k"), AX.X, ALU.add)
            last.then_inc(gates_ready, 1)
            dve.wait_ge(cum_pe, 1)
            link(v.scalar_tensor_tensor(rank[:, :, 0:E], grid(bank[5][:, 0:TT * E], TT, E), 1.0, mask, ALU.add, ALU.mult))
            link(v.tensor_scalar(rank[:, :, 0:E], rank[:, :, 0:E], -1.0, None, ALU.add))
            over_f, upto, before_f = numf[:, 0:E], numf[:, E + 1:2 * E + 1], numf[:, 2 * E + 1:3 * E + 1]
            link(v.tensor_scalar(over_f, bank[6][0:1, 0:E], float(CAP), None, ALU.is_gt))
            link(v.tensor_tensor_scan(upto, over_f, over_f, 0.0, ALU.add, ALU.bypass))
            link(v.tensor_tensor(before_f, upto, over_f, ALU.subtract))
            v.tensor_copy(nums[:, 0:E], over_f)
            v.tensor_copy(nums[:, E:2 * E], before_f)
            v.tensor_copy(nums[:, 2 * E:2 * E + 1], upto[:, E - 1:E]).then_inc(nums_ready, 1)

            def picks(e, slot, buf):
                for t in range(TT):
                    v.tensor_scalar(pick[:, t, :], slot, rank[:, t, bass.ds(e, 1)], None, ALU.is_equal)
                return v.tensor_copy(onehot[:, buf, :], esel[:, bass.ds(e, 1)].to_broadcast([96, CAP]))

            def spreads(e, slot):
                both = slot.unsqueeze(1).to_broadcast([128, 2, CAP])
                for t in range(TT):
                    last = v.tensor_scalar(spread[:, t, :, :], both, rank[:, t, bass.ds(e, 1)], gate[:, t, bass.ds(e, 1)],
                                           ALU.is_equal, ALU.mult)
                return last

            def clip_gate():
                return v.tensor_scalar(gc, bank[4][:, :], 7.0, None, ALU.min)

            def clip_lin():
                return v.tensor_scalar(lc, bank[5][:, :], 7.0, -7.0, ALU.min, ALU.max)

            def lin_times_gate():
                return v.scalar_tensor_tensor(lc, lc, 1.0, gc, ALU.add, ALU.mult)

            def times_sigmoid():
                return v.tensor_tensor(lc, lc, sg, ALU.mult)

            first = iota[:, 0:CAP]
            dve.wait_ge(consts, 9)
            dve.wait_ge(gmT_sb, 1)
            dve.wait_ge(nums_ready, 1)
            v.memset(yrow, 0.0).then_inc(y_row, 1)
            picks(0, first, 0).then_inc(pick_ready, 1)
            any_more = dve.value_load(nums[0:1, 2 * E:2 * E + 1], min_val=0, max_val=E)
            with dve.Fori(0, E // 2) as i:
                for half in range(2):
                    e = i * 2 + half
                    dve.wait_ge(h_pe, e + 1)
                    picks(e + 1, first, 1 - half).then_inc(pick_ready, 1)
                    dve.wait_ge(chunk_used, e * PER + KD)
                    clip_gate().then_inc(g_clip, 1)
                    clip_lin().then_inc(lin_ready, 1)
                    spreads(e, first).then_inc(spread_ready, 1)
                    dve.wait_ge(lin_ready, e + 1)
                    lin_times_gate().then_inc(swi, 1)
                    dve.wait_ge(swi, e + 1)
                    dve.wait_ge(g_sig, e + 1)
                    times_sigmoid().then_inc(act_ready, 1)
                    with dve.If(any_more > 0):
                        over = dve.value_load(nums[0:1, bass.ds(e, 1)], min_val=0, max_val=1)
                        with dve.If(over > 0):
                            before = dve.value_load(nums[0:1, bass.ds(e + E, 1)], min_val=0, max_val=E)
                            with dve.Fori(0, MORE) as b:
                                o = before * MORE_STEPS + b * BLOCK_STEPS
                                slot = iota[:, bass.ds(b * CAP + CAP, CAP)]
                                dve.wait_ge(step, o + 1)
                                picks(e, slot, half)
                                spreads(e, slot).then_inc(step, 1)
                                dve.wait_ge(step, o + 7)
                                clip_lin()
                                clip_gate().then_inc(step, 1)
                                dve.wait_ge(step, o + 9)
                                lin_times_gate().then_inc(step, 1)
                                dve.wait_ge(step, o + 10)
                                times_sigmoid().then_inc(step, 1)
                            a = before * MORE_STEPS + MORE * BLOCK_STEPS
                            dve.wait_ge(step, a + 1)
                            v.memset(yrow, 0.0)
                            picks(e + 1, first, 1 - half).then_inc(step, 1)
                            dve.wait_ge(step, a + 6)
                            dve.sem_inc(passed, 1)
            dve.wait_ge(fin_in, 16)
            for t in range(TT):
                dve.wait_ge(x2_sq, t + 1)
                row_var(t).then_inc(var_f, 1)
                dve.wait_ge(std_f, t + 1)
                normed(t, at(1 + t, D), at(0, D)).then_inc(o_ready, 1)

        @block.tensor
        def _(pe):
            mm, tr = nc.tensor.matmul, nc.tensor.transpose
            pe.wait_ge(consts, 1)
            pe.wait_ge(par_in, 16 * 9)
            pe.wait_ge(ls_rows, 1)
            pe.wait_ge(tap_in, 16)
            tr(bank[0][:, 0:54], par_rows[:, :], ident[0:54, 0:54])
            for k in range(KC):
                last = tr(bank[0][:, 64 + k * W:64 + k * W + W], tap_rows[:, k * 128:k * 128 + 128], ident[0:W, 0:W])
            last.then_inc(params_pe, 1)
            pe.wait_ge(xr_ready, TT)
            for k in range(KD):
                for t in range(TT):
                    last = tr(bank[4 + k // 2][:, (k % 2) * T + t * 128:(k % 2) * T + t * 128 + 128],
                              xr[:, t, k * 128:k * 128 + 128], ident[:, :])
                if k % 2:
                    last.then_inc(xT_pe, 1)

            ACT_TAKES = {n: i + 1 for i, n in enumerate([0, 2, 4, 5] + list(range(7, NCH)))}
            DVE_TAKES = {1: 1, 3: 2, 6: 3}

            def freed(n):
                if n in DVE_TAKES:
                    pe.wait_ge(win_dve, DVE_TAKES[n])
                else:
                    pe.wait_ge(win_act, ACT_TAKES[n])

            def project(n):
                if n >= 4:
                    freed(n - 4)
                pe.wait_ge(win_in[n % WRING], 16 * (n // WRING + 1))
                w = grid(at(n % WRING, CH), KD, 256)
                for m in range(2):
                    for k in range(KD):
                        last = mm(bank[4 + n % 4][:, m * T:m * T + T], w[:, k, m * 128:m * 128 + 128], hT[:, k, :],
                                  start=(k == 0), stop=(k == KD - 1))
                last.then_inc(win_pe, 1)

            def raw_transpose(raw, n0):
                for n in range(4):
                    for q in range(4):
                        last = tr(bank[n][:, q * 128:q * 128 + 128], raw[:, q % 2, 2 * n + q // 2, :], ident[:, :])
                    last.then_inc(rawT_pe, 1)

            def bu_mm(t):
                if t >= 2:
                    pe.wait_ge(bu_sb, t - 1)
                for ri in range(2):
                    last = mm(bank[t % 2][:, ri * T:ri * T + T], bT[:, t, ri, :], uT[:, t // 4, :], start=True, stop=True)
                last.then_inc(bu_pe, 1)

            def y_mm(t):
                pe.wait_ge(states, t + 1)
                for ri in range(2):
                    last = mm(bank[3][:, t // 4 * T:t // 4 * T + T], cT[:, t, ri, :], xs[t % 2][:, ri, :],
                              start=(t % 4 == 0 and ri == 0), stop=(t % 4 == 3 and ri == 1))
                last.then_inc(y_pe, 1)

            pe.wait_ge(hT_ready, KD)
            project(0)
            project(1)
            pe.wait_ge(raw_ready, 1)
            pe.wait_ge(params_sb, 2)
            raw_transpose(craw, 0)
            project(2)
            project(3)
            pe.wait_ge(raw_ready, 2)
            pe.wait_ge(rawT_sb, 4)
            raw_transpose(braw, 4)
            project(4)
            project(5)
            pe.wait_ge(rawT_sb, 8)
            freed(4)
            for t in range(4):
                bu_mm(t)
            project(6)
            project(7)
            for n, ts, bs in ((8, (), (4, 5)), (9, (0, 1), ()), (10, (2, 3), (6, 7)), (11, (4, 5), ()), (12, (6, 7), ())):
                for t in ts:
                    y_mm(t)
                for t in bs:
                    bu_mm(t)
                project(n)
            project(13)
            pe.wait_ge(consts, 8)
            pe.wait_ge(conv_done, KC)
            pe.wait_ge(bu_sb, ST)
            for k in range(KC):
                last = mm(bank[0][:, 0:T], ones, conv[:, k, :], start=(k == 0), stop=(k == KC - 1))
            last.then_inc(mean_pe, 1)
            project(14)
            pe.wait_ge(y_gelu, 1)
            pe.wait_ge(glu_in, 16)
            for m in range(2):
                for k in range(2):
                    last = mm(bank[2][:, m * T:m * T + T], wglu[:, k, m * 128:m * 128 + 128], ygelu[:, k, :],
                              start=(k == 0), stop=(k == 1))
            last.then_inc(glu_pe, 1)
            for k in range(KC):
                pe.wait_ge(conv_sq, k + 1)
                last = mm(bank[1][:, 0:T], ones, silu[:, k, :], start=(k == 0), stop=(k == KC - 1))
            last.then_inc(var_pe, 1)
            pe.wait_ge(y_glu, 1)
            pe.wait_ge(wssm_in, 16)
            for j in range(4):
                b = (2, 3, 0, 1)[j]
                if b == 1:
                    pe.wait_ge(var_c, 1)
                for m in range(2):
                    c = (2 * j + m) * 128
                    for k in range(2):
                        last = mm(bank[b][:, m * T:m * T + T], wssm[:, k, c:c + 128], yglu[:, k, :],
                                  start=(k == 0), stop=(k == 1))
                last.then_inc(ssm_pe, 1)
            pe.wait_ge(wconv_in, 16)
            for j in range(4):
                freed(11 + j if j else 12)
                if j == 0:
                    freed(14)
                for m in range(2):
                    c = (2 * j + m) * 128
                    for k in range(KC):
                        if j == 0 and m == 0:
                            pe.wait_ge(silu_ready, k + 1)
                        last = mm(bank[4 + j][:, m * T:m * T + T], wconv[:, k, c:c + 128], silu[:, k, :],
                                  start=(k == 0), stop=(k == KC - 1))
                last.then_inc(conv_pe, 1)
                if j == 1:
                    pe.wait_ge(ssm_gated, 4)
                    for n in range(4):
                        mm(bank[n][:, :], ident[:, :], x_sb[:, n // 2, n % 2 * 512:n % 2 * 512 + 512], start=True, stop=False)
            pe.wait_ge(wout_in, 16)
            for t in range(TT):
                for k in range(KD):
                    pe.wait_ge(mixed, k // 2 + 1)
                    for h in range(2):
                        last = mm(bank[2 * t + h][:, :], gateC[:, k, t * 128:t * 128 + 128], wout[:, k, h * 512:h * 512 + 512],
                                  start=False, stop=(k == KD - 1))
                    if t == 1 and k % 2:
                        last.then_inc(wout_used, 1)
                if t == 0:
                    last.then_inc(x1_pe, 1)
            pe.wait_ge(ffn_in, 48)
            for t in range(TT):
                pe.wait_ge(h_ready, t + 1)
                for k in range(KD):
                    last = tr(bank[4 + 2 * t + k // 4][:, k % 4 * 128:k % 4 * 128 + 128],
                              rows[:, t, k * 128:k * 128 + 128], ident[:, :])
                    if k % 4 == 3:
                        last.then_inc(h2T_pe, 1)
            for t in range(TT):
                pe.wait_ge(h2T_act, t + 1)
                pe.wait_ge(h2T_dve, t + 1)
                for k in range(KD):
                    mm(bank[4 + 2 * t][:, 0:E], h2T[:, t, k, :], wrt[:, k, :], start=(k == 0), stop=False)
                mm(bank[4 + 2 * t][:, 0:E], ones[0:1, :], brow[:, :], start=False, stop=True).then_inc(logits_pe, 1)
            pe.wait_ge(consts, 9)
            pe.wait_ge(mask_ready, 1)
            pe.wait_ge(top8, TT)
            mm(bank[5][:, 0:E], tri, mask[:, 0, :], start=True, stop=True)
            mm(bank[5][:, E:2 * E], ones, mask[:, 0, :], start=True, stop=False)
            mm(bank[5][:, E:2 * E], tri, mask[:, 1, :], start=False, stop=True)
            mm(bank[6][0:1, 0:E], ones[:, 0:1], mask[:, 0, :], start=True, stop=False)
            mm(bank[6][0:1, 0:E], ones[:, 0:1], mask[:, 1, :], start=False, stop=True).then_inc(cum_pe, 1)
            pe.wait_ge(gates_ready, 1)
            for t in range(TT):
                last = tr(bank[7][0:E, t * 128:t * 128 + 128], gate[:, t, 0:E], ident[:, :])
            last.then_inc(gmT_pe, 1)
            pe.wait_ge(gmT_sb, 1)
            pe.wait_ge(down_in, 16)
            for n in range(4):
                last = mm(bank[n][:, :], gmT[:, n // 2 * 128:n // 2 * 128 + 128], bdown[:, n % 2 * 512:n % 2 * 512 + 512],
                          start=False, stop=False, skip_group_check=True)
            last.then_inc(bdown_pe, 1)

            def gather():
                for t in range(TT):
                    for h in range(2):
                        last = mm(bank[6][64 * h:64 * h + 64, :], pick[:, t, :], rows[:, t, h * 512:h * 512 + 512],
                                  start=(t == 0), stop=(t == TT - 1))
                return last

            def transposes(src):
                for m in range(4):
                    last = tr(bank[7][:, m * 128:m * 128 + 128], src[:, m * 128:m * 128 + 128], ident[:, :])
                return last

            def spread_transposes():
                for t in range(TT):
                    last = tr(bank[6][:, t * 128:t * 128 + 128], spread[:, t, :, :].rearrange("p a b -> p (a b)"), ident[:, :])
                return last

            def gate_up(half, buf, uses=None):
                for b in range(2):
                    for h in range(2):
                        mm(bank[4 + b][64 * h:64 * h + 64, :], onehot[:, buf, :], biasb[:, (2 * b + h) * 512:(2 * b + h + 1) * 512],
                           start=True, stop=False)
                for k in range(KD):
                    if uses is not None:
                        pe.wait_ge(slot_in[half * PER + k], uses)
                    w = at(half * PER + k, CH)
                    for b in range(2):
                        for h in range(2):
                            last = mm(bank[4 + b][64 * h:64 * h + 64, :], heT[:, k % 4, k // 4 * 64:k // 4 * 64 + 64],
                                      w[:, b * FF + h * 512:b * FF + h * 512 + 512], start=False, stop=(k == KD - 1))
                    if uses is not None:
                        last.then_inc(chunk_used, 1)
                return last

            def down(half, uses=None):
                for k in range(KD):
                    if uses is not None and k % 2 == 0:
                        pe.wait_ge(slot_in[half * PER + KD + k // 2], uses)
                    w = grid(at(half * PER + KD + k // 2, CH), 2, D)
                    for h in range(2):
                        last = mm(bank[6][64 * h:64 * h + 64, :], actT[:, k % 4, k // 4 * 64:k // 4 * 64 + 64],
                                  w[:, k % 2, h * 512:h * 512 + 512], start=(k == 0), stop=(k == KD - 1))
                    if uses is not None and k % 2:
                        last.then_inc(chunk_used, 1)
                return last

            def scatter():
                for n in range(4):
                    last = mm(bank[n][:, :], spT[:, n % 2, n // 2, :], yrow, start=False, stop=False, skip_group_check=True)
                return last

            pe.wait_ge(pick_ready, 1)
            gather().then_inc(h_pe, 1)
            pe.wait_ge(h_row, 1)
            transposes(hrow).then_inc(hT_pe, 1)
            pe.wait_ge(nums_ready, 1)
            any_more = pe.value_load(nums[0:1, 2 * E:2 * E + 1], min_val=0, max_val=E)
            with pe.Fori(0, E // 2) as i:
                for half in range(2):
                    e = i * 2 + half
                    pe.wait_ge(h_T, e + 1)
                    gate_up(half, half, i * 16 + 16)
                    pe.wait_ge(pick_ready, e + 2)
                    pe.wait_ge(y_row, e + 1)
                    gather().then_inc(h_pe, 1)
                    scatter()
                    pe.wait_ge(h_row, e + 2)
                    transposes(hrow).then_inc(hT_pe, 1)
                    pe.wait_ge(spread_ready, e + 1)
                    spread_transposes().then_inc(spT_pe, 1)
                    pe.wait_ge(act_ready, e + 1)
                    pe.wait_ge(h_T, e + 2)
                    transposes(lc).then_inc(aT_pe, 1)
                    pe.wait_ge(spT_sb, e + 1)
                    pe.wait_ge(a_T, e + 1)
                    down(half, i * 16 + 16)
                    with pe.If(any_more > 0):
                        over = pe.value_load(nums[0:1, bass.ds(e, 1)], min_val=0, max_val=1)
                        with pe.If(over > 0):
                            before = pe.value_load(nums[0:1, bass.ds(e + E, 1)], min_val=0, max_val=E)
                            pe.wait_ge(y_row, e + 2)
                            pe.sem_inc(passed, 1)
                            with pe.Fori(0, MORE) as b:
                                o = before * MORE_STEPS + b * BLOCK_STEPS
                                pe.wait_ge(step, o)
                                scatter().then_inc(step, 1)
                                pe.wait_ge(step, o + 2)
                                gather().then_inc(step, 1)
                                pe.wait_ge(step, o + 4)
                                transposes(hrow)
                                spread_transposes().then_inc(step, 1)
                                pe.wait_ge(step, o + 6)
                                gate_up(half, half).then_inc(step, 1)
                                pe.wait_ge(step, o + 11)
                                transposes(lc).then_inc(step, 1)
                                pe.wait_ge(step, o + 13)
                                down(half).then_inc(step, 1)
                            a = before * MORE_STEPS + MORE * BLOCK_STEPS
                            pe.wait_ge(step, a)
                            scatter().then_inc(step, 1)
                            pe.wait_ge(step, a + 2)
                            gather().then_inc(step, 1)
                            pe.wait_ge(step, a + 4)
                            transposes(hrow).then_inc(step, 1)
                            pe.wait_ge(step, a + 6)
                            pe.sem_inc(passed, 1)
            pe.wait_ge(y_row, E + 1)
            for t in range(TT):
                for h in range(2):
                    last = mm(bank[2 * t + h][:, :], spT[:, h, t, :], yrow, start=False, stop=True, skip_group_check=True)
                last.then_inc(x2_pe, 1)


_INS = ["x", "norm_mix_g", "w_in", "conv_w", "conv_b", "conv_ln_g", "conv_ln_b", "w_conv_out",
        "ssm_a_re", "ssm_a_im", "ssm_log_step", "ssm_b_re", "ssm_b_im", "ssm_c_re", "ssm_c_im", "ssm_d",
        "w_ssm_glu", "b_ssm_glu", "w_ssm_out", "w_out", "norm_ffn_g", "w_router", "b_router",
        "w_gate_up", "b_gate_up", "w_down", "b_down", "norm_final_g"]


def kernel(**inputs):
    import concourse.bacc as bacc
    from concourse.bass_utils import run_bass_kernel_spmd

    nc = bacc.Bacc("TRN2", target_bir_lowering=False, num_devices=1, dynamic_dma_scratch_size=64)
    arrays = {n: np.ascontiguousarray(inputs[n]) for n in _INS}
    args = [nc.dram_tensor(n, arrays[n].shape, F32, kind="ExternalInput").ap() for n in _INS]
    out = nc.dram_tensor("out", (1, T, D), F32, kind="ExternalOutput").ap()
    build(nc, *args, out)
    r = run_bass_kernel_spmd(nc, [arrays], core_ids=[0])
    return r.results[0]["out"]
```

```python
import numpy as np
import concourse.bass as bass
from concourse import mybir
from contextlib import ExitStack

F32 = mybir.dt.float32
BF16 = mybir.dt.bfloat16
I32 = mybir.dt.int32
U32 = mybir.dt.uint32
ALU = mybir.AluOpType
ACT = mybir.ActivationFunctionType
AX = mybir.AxisListType

D = 1024
T = 256
TT = T // 128
KD = D // 128
DC = 768
KC = DC // 128
W = 31
DS = 256
G, P, H = 16, 64, 16
ST = G * P // 128
E = 32
TOPK = 4
FF = 1024
CAP = 64
MORE = T // CAP - 1
EPS = 1e-6
CH = 2048
SLOTS = 24
PER = 12
NCH = 15
WRING = 6
ORDER = [3, 0, 4, 1, 6, 5, 2] + list(range(7, 15))
TWO_PI = 6.283185307179586
C1 = 6.28125
C2 = float(np.float32(np.round((TWO_PI - C1) * 2 ** 20) / 2 ** 20))
C3 = float(TWO_PI - C1 - C2)
ROUND = 12582912.0
SCAN_TAPS = 4
WARM = 4, 8
LEVELS = 8
BLOCK_STEPS = 15
AGAIN_STEPS = 6
MORE_STEPS = MORE * BLOCK_STEPS + AGAIN_STEPS


def build(nc, x, norm_mix_g, w_in, conv_w, conv_b, conv_ln_g, conv_ln_b, w_conv_out,
          ssm_a_re, ssm_a_im, ssm_log_step, ssm_b_re, ssm_b_im, ssm_c_re, ssm_c_im, ssm_d,
          w_ssm_glu, b_ssm_glu, w_ssm_out, w_out, norm_ffn_g, w_router, b_router,
          w_gate_up, b_gate_up, w_down, b_down, norm_final_g, out):
    with ExitStack() as ctx:
        def sb(name, shape, dt=F32):
            return ctx.enter_context(nc.sbuf_tensor(name, shape, dt))

        def sem(name):
            return ctx.enter_context(nc.semaphore(name))

        ring = sb("ring", [128, SLOTS * CH])

        def at(slot, n, off=0):
            return ring[:, slot * CH + off:slot * CH + off + n]

        def grid(ap, *dims):
            names = "abcd"[:len(dims)]
            sizes = {c: d for c, d in zip(names[1:], dims[1:])}
            return ap.rearrange(f"p ({' '.join(names)}) -> p {' '.join(names)}", **sizes)

        wconv = grid(at(6, 3 * CH), KC, D)
        wssm = grid(at(12, CH), 2, D)
        wout = grid(at(13, 4 * CH), KD, D)
        wglu = grid(at(22, 512, 1536), 2, DS)
        cosT, sinT = grid(at(9, CH), ST, T), grid(at(10, CH), ST, T)
        braw = grid(at(11, 512), 2, 2, 128)
        bu = [grid(at(11, 512, 512 * i), 2, T) for i in range(2)]
        wz = [grid(at(11, 512, 1024 + 512 * i), 2, T) for i in range(2)]
        ygelu, yglu = grid(at(11, 512), 2, T), grid(at(11, 512, 512), 2, T)
        squares = grid(at(17, CH), TT, D)
        gateC = grid(at(17, CH), KD, T)
        gateS = grid(at(18, CH), KD, T)
        tab_tmp = at(18, 1024), at(18, 1024, 1024)
        bias32 = ring[0:96, 16 * CH:17 * CH]
        bT = grid(at(20, 512, 512), 2, 2, 128)
        cT = grid(at(20, 512), 2, 2, 128)
        PADT = T + W - 1
        vT = grid(at(21, KC * PADT), KC, PADT)
        silu = grid(at(21, KC * T), KC, T)
        conv = grid(at(22, KC * T), KC, T)
        craw = grid(at(23, 512), 2, 2, 128)
        q_dve = grid(at(23, 512), 2, T)
        zz = grid(at(23, 512, 512), 2, T)
        xs = [grid(at(19, 512, 512 * i), 2, T) for i in range(4)] + \
             [grid(at(23, 512, 1024 + 512 * i), 2, T) for i in range(2)]
        NX = len(xs)
        h2T = grid(at(18, CH), TT, KD, 128)
        gffn = at(19, D)
        lg = grid(at(20, 64, 1280), TT, E)
        sel = grid(at(20, 256, 1344), TT * TOPK, E)
        mask = grid(at(20, 64, 1600), TT, E)
        v8 = grid(at(20, 16, 1664), TT, 8)
        idx8 = grid(at(20, 16, 1680), TT, 8).bitcast(U32)
        idxf = grid(at(20, 16, 1696), TT, 8)
        pe4 = grid(at(20, 8, 1712), TT, TOPK)
        gmT = ring[0:E, 20 * CH + 1728:20 * CH + 1728 + T]
        wrt = grid(at(19, KD * E, D), KD, E)
        bdown = ring[0:E, 20 * CH:20 * CH + D]
        tri, ones = at(20, 128, 1024), at(20, 128, 1152)
        rows = sb("rows", [128, TT, D])
        x_sb = rows
        area = sb("area", [128, 3584])
        hT = grid(area[:, 0:2048], KD, T)
        uT = grid(area[:, 2048:2560], 2, T)
        q_pool = grid(area[:, 2560:3072], 2, T)
        ones_1, diag = area[:, 2560:2688], grid(area[:, 2688:2944], TT, 128)
        rstd_all = area[:, 3072:3328]
        sig_a = grid(area[:, 3072:3584], 2, T)
        mean, rstdc = area[:, 3072:3328], area[:, 3328:3584]
        gc, sg, lc = area[:, 0:512], area[:, 512:1024], area[:, 1024:1536]
        actT = grid(area[:, 1536:2048], 4, 128)
        hrow, yrow = area[:, 2048:2560], area[:, 2560:3072]
        heT = grid(area[:, 3072:3584], 4, 128)
        ident = sb("ident", [128, 128])
        iota = sb("iota", [128, T], BF16)
        rank = sb("rank", [128, TT, E + 1])
        gate = sb("gate", [128, TT, E + 1])
        pick = sb("pick", [128, TT, CAP])
        spread = sb("spread", [128, TT, 2, CAP])
        spT = sb("spT", [128, 2, TT, 128])
        biasb = sb("biasb", [96, 4 * 512], BF16)
        esel = sb("esel", [96, E + 1], BF16)
        onehot = sb("onehot", [96, 2, CAP], BF16)
        nums = sb("nums", [1, 2 * E + 1], I32)
        numf = spread[0:1, :, :, :].rearrange("p t d s -> p (t d s)")[:, 0:3 * E + 1]
        late = spread[:, :, :, :].rearrange("p t d s -> p (t d s)")
        par = late[:, 0:54]
        taps = grid(late[:, 54:54 + KC * W], KC, W)
        mag = late[:, 240:248]
        par_rows = ring[0:54, 12 * CH:12 * CH + 128]
        tap_rows = at(22, DC)[0:W, :]
        ssb = grid(at(12, 256, 128), 2, ST, H)
        bbar = grid(at(12, 256, 384), 2, ST, H)
        btmp = grid(at(12, 128, 640), ST, H)
        pw = grid(at(12, LEVELS * 2 * ST, 768), LEVELS, 2, ST)
        brow = ring[0:1, 19 * CH + 1984:19 * CH + 1984 + E]
        sm = sb("sm", [128, 12])
        cld = grid(at(22, 256, 1024), 2, 2, P)
        gmask = at(12, 8, 1000)
        gpairs = at(12, 4, 1008)
        pmask = grid(at(12, 4, 996), 2, 2)
        hmask = at(12, 2, 1016)

        bank = [ctx.enter_context(nc.psum_tensor(f"bank{i}", [128, 512], F32)) for i in range(8)]

        p_ls, p_g, p_cb, p_lg, p_lb = par[:, 0:8], par[:, 8:16], par[:, 16:22], par[:, 22:28], par[:, 28:34]
        p_d, p_bg, p_re, p_im = par[:, 34:36], par[:, 36:38], par[:, 38:46], par[:, 46:54]
        log_steps = ring[0:ST, 12 * CH + 1018:12 * CH + 1020]
        ss, rstd, ss4 = sm[:, 0:2], sm[:, 2:4], sm[:, 4:8]
        top_sum, neg_top = sm[:, 8:10], sm[:, 10:12]
        dt8, th, lrdt, kk, rr, ra, den, t1, t2, fr, fi, pool_tmp = (at(12, ST, 900 + ST * n) for n in range(12))

        x_in = [sem(f"x_in{t}") for t in range(TT)]
        par_in = sem("par_in")
        tap_in = sem("tap_in")
        ls_rows = sem("ls_rows")
        ssm_in = sem("ssm_in")
        c_in = sem("c_in")
        bias_in = sem("bias_in")
        glu_in = sem("glu_in")
        win_in = [sem(f"win_in{i}") for i in range(WRING)]
        wconv_in = sem("wconv_in")
        wssm_in = sem("wssm_in")
        wout_in = sem("wout_in")
        ffn_in = sem("ffn_in")
        down_in = sem("down_in")
        fin_in = sem("fin_in")
        slot_in = [sem(f"slot_in{i}") for i in range(SLOTS)]
        stored = sem("stored")
        dve_own = sem("dve_own")
        pool_own = sem("pool_own")
        consts = sem("consts")
        params_pe = sem("params_pe")
        params_sb = sem("params_sb")
        x_sq = sem("x_sq")
        var_x = sem("var_x")
        std_x = sem("std_x")
        ones_ready = sem("ones_ready")
        diag_ready = sem("diag_ready")
        spread_pe = sem("spread_pe")
        rstd_sb = sem("rstd_sb")
        hT_ready = sem("hT_ready")
        act_dt = sem("act_dt")
        dve_th = sem("dve_th")
        act_mag = sem("act_mag")
        dve_rr = sem("dve_rr")
        act_sin = sem("act_sin")
        dve_f = sem("dve_f")
        tables = sem("tables")
        raw_ready = sem("raw_ready")
        rawT_pe = sem("rawT_pe")
        rawT_sb = sem("rawT_sb")
        win_pe = sem("win_pe")
        win_act = sem("win_act")
        win_dve = sem("win_dve")
        bu_pe = sem("bu_pe")
        bu_sb = sem("bu_sb")
        turned = sem("turned")
        scanned = sem("scanned")
        states = sem("states")
        y_pe = sem("y_pe")
        y_pre = sem("y_pre")
        y_gelu = sem("y_gelu")
        glu_pe = sem("glu_pe")
        glu_sig = sem("glu_sig")
        y_glu = sem("y_glu")
        conv_done = sem("conv_done")
        mean_pe = sem("mean_pe")
        centred = sem("centred")
        conv_sq = sem("conv_sq")
        var_pe = sem("var_pe")
        var_c = sem("var_c")
        std_c = sem("std_c")
        scaled = sem("scaled")
        silu_ready = sem("silu_ready")
        ssm_pe = sem("ssm_pe")
        ssm_gated = sem("ssm_gated")
        conv_pe = sem("conv_pe")
        mixed = sem("mixed")
        x1_pe = sem("x1_pe")
        wout_used = sem("wout_used")
        x1_sq = sem("x1_sq")
        var_h = sem("var_h")
        std_h = sem("std_h")
        h_ready = sem("h_ready")
        h2T_pe = sem("h2T_pe")
        h2T_act = sem("h2T_act")
        h2T_dve = sem("h2T_dve")
        logits_pe = sem("logits_pe")
        top8 = sem("top8")
        probs = sem("probs")
        mask_ready = sem("mask_ready")
        cum_pe = sem("cum_pe")
        gates_ready = sem("gates_ready")
        gmT_pe = sem("gmT_pe")
        gmT_sb = sem("gmT_sb")
        bdown_pe = sem("bdown_pe")
        nums_ready = sem("nums_ready")
        biasb_ready = sem("biasb_ready")
        pick_ready = sem("pick_ready")
        h_pe = sem("h_pe")
        h_row = sem("h_row")
        hT_pe = sem("hT_pe")
        h_T = sem("h_T")
        chunk_used = sem("chunk_used")
        g_clip = sem("g_clip")
        g_sig = sem("g_sig")
        act_ready = sem("act_ready")
        spT_pe = sem("spT_pe")
        spT_sb = sem("spT_sb")
        aT_pe = sem("aT_pe")
        a_T = sem("a_T")
        y_row = sem("y_row")
        spread_ready = sem("spread_ready")
        lin_ready = sem("lin_ready")
        swi = sem("swi")
        passed = sem("passed")
        step = sem("step")
        x2_pe = sem("x2_pe")
        x2_sq = sem("x2_sq")
        var_f = sem("var_f")
        std_f = sem("std_f")
        o_ready = sem("o_ready")

        block = ctx.enter_context(nc.Block())

        win_v = w_in[0].rearrange("(k p) n -> p k n", p=128)
        gu_v = w_gate_up[0].rearrange("e (k p) n -> e k p n", p=128)
        dn_v = w_down[0].rearrange("e (c k p) n -> e c p k n", k=2, p=128)

        @block.sync
        def _(sp):
            for t in range(TT):
                sp.dma_start(x_sb[:, t, :], x[0, t * 128:t * 128 + 128, :]).then_inc(x_in[t], 16)
            sp.dma_start(log_steps, ssm_log_step[0].rearrange("(t g) -> t g", g=2)).then_inc(par_in, 16)
            r0 = ST
            for src, n in ((norm_mix_g, 8), (conv_b, 6), (conv_ln_g, 6), (conv_ln_b, 6), (ssm_d, 2), (b_ssm_glu, 2)):
                sp.dma_start(par_rows[r0:r0 + n, :], src[0].rearrange("(k p) -> k p", p=128)).then_inc(par_in, 16)
                r0 += n
            for src in (ssm_a_re, ssm_a_im):
                sp.dma_start(par_rows[r0:r0 + ST, :], src[0].rearrange("(t g) p -> t (g p)", g=2)).then_inc(par_in, 16)
                r0 += ST

            def load_win(c):
                if c >= WRING:
                    sp.wait_ge(win_pe, c - WRING + 1)
                sp.dma_start(grid(at(c % WRING, CH), KD, 256),
                             win_v[:, :, ORDER[c] * 256:ORDER[c] * 256 + 256]).then_inc(win_in[c % WRING], 16)

            load_win(0)
            sp.dma_start(tap_rows, conv_w[0]).then_inc(tap_in, 16)
            for ri, src in enumerate((ssm_c_re, ssm_c_im)):
                sp.dma_start(cld[:, ri, :, :], src[0].rearrange("(c g) h p -> (g h) c p", c=2)).then_inc(c_in, 16)
            for ri, src in enumerate((ssm_b_re, ssm_b_im)):
                sp.dma_start(ssb[:, ri, :, :], src[0].rearrange("(t g) p h -> (g p) t h", g=2)).then_inc(ssm_in, 16)

            load_win(1)
            for n in range(3):
                sp.dma_start(bias32[32 * n:32 * n + 32, :], b_gate_up[0]).then_inc(bias_in, 16)
            for c in range(2, WRING):
                load_win(c)
            sp.dma_start(wglu, w_ssm_glu[0].rearrange("(k p) n -> p k n", p=128)).then_inc(glu_in, 16)
            for c in range(WRING, NCH):
                load_win(c)
            sp.dma_start(wconv, w_conv_out[0].rearrange("(k p) n -> p k n", p=128)).then_inc(wconv_in, 16)
            sp.wait_ge(tables, 1)
            sp.wait_ge(dve_f, 1)
            sp.dma_start(wssm, w_ssm_out[0].rearrange("(k p) n -> p k n", p=128)).then_inc(wssm_in, 16)

            def load(e, j, half):
                if j < KD:
                    src, dst = gu_v[e, j], at(half * PER + j, CH)
                else:
                    src, dst = dn_v[e, j - KD], grid(at(half * PER + j, CH), 2, D)
                sp.dma_start(dst, src).then_inc(slot_in[half * PER + j], 16)

            sp.wait_ge(y_pe, ST)
            sp.dma_start(gffn, norm_ffn_g.to_broadcast([128, D])).then_inc(ffn_in, 16)
            sp.dma_start(wrt, w_router[0].rearrange("(k p) n -> p k n", p=128)).then_inc(ffn_in, 16)
            sp.dma_start(brow, b_router).then_inc(ffn_in, 16)
            sp.dma_start(bdown, b_down[0]).then_inc(down_in, 16)
            sp.wait_ge(states, ST)
            load(1, 11, 1)
            load(0, 9, 0)
            load(0, 10, 0)

            def load_over_win(js):
                for j in js:
                    sp.wait_ge(win_pe, NCH - WRING + (j - (NCH - WRING)) % WRING + 1)
                    load(0, j, 0)

            load_over_win((3, 4, 5, 0))
            sp.wait_ge(biasb_ready, 1)
            sp.dma_start(wout, w_out[0].rearrange("(k p) n -> p k n", p=128)).then_inc(wout_in, 16)
            load_over_win((1, 2))
            sp.wait_ge(silu_ready, KC)
            load(1, 10, 1)
            sp.wait_ge(ssm_pe, 4)
            load(0, 11, 0)
            load(1, 0, 1)
            sp.wait_ge(conv_pe, 4)
            for j in (6, 7, 8):
                load(0, j, 0)
            load(1, 9, 1)
            for j in (1, 2, 3, 4):
                sp.wait_ge(wout_used, j)
                load(1, j, 1)
            load(1, 5, 1)
            sp.wait_ge(logits_pe, TT)
            load(1, 6, 1)
            load(1, 7, 1)
            sp.wait_ge(bdown_pe, 1)
            sp.wait_ge(pick_ready, 1)
            load(1, 8, 1)
            sp.wait_ge(nums_ready, 1)
            any_more = sp.value_load(nums[0:1, 2 * E:2 * E + 1], min_val=0, max_val=E)
            with sp.Fori(0, E // 2 - 1) as i:
                for half in range(2):
                    e = i * 2 + half
                    with sp.If(any_more > 0):
                        over = sp.value_load(nums[0:1, bass.ds(e, 1)], min_val=0, max_val=1)
                        with sp.If(over > 0):
                            before = sp.value_load(nums[0:1, bass.ds(e + E, 1)], min_val=0, max_val=E)
                            sp.wait_ge(step, before * MORE_STEPS + MORE_STEPS + 1)
                            sp.sem_inc(passed, 1)
                    for j in range(PER):
                        sp.wait_ge(chunk_used, e * PER + j + 1)
                        load(e + 2, j, half)
            sp.wait_ge(chunk_used, E * PER - PER)
            sp.dma_start(at(0, D), norm_final_g.unsqueeze(0).to_broadcast([128, D])).then_inc(fin_in, 16)
            for t in range(TT):
                for h in range(2):
                    sp.wait_ge(o_ready, 2 * t + h + 1)
                    sp.dma_start(out[0, t * 128:t * 128 + 128, h * 512:h * 512 + 512], at(1 + t, 512, h * 512)).then_inc(stored, 16)
            sp.wait_ge(stored, 16 * 2 * TT)

        @block.gpsimd
        def _(pool):
            own = [0]

            def link(ins):
                own[0] += 1
                ins.then_inc(pool_own, 1)
                pool.wait_ge(pool_own, own[0])

            g = nc.gpsimd
            link(g.memset(ident[:, :], 0.0))
            g.affine_select(out=ident[:, :], in_=ident[:, :], compare_op=ALU.not_equal, fill=1.0, base=0,
                            pattern=[[-1, 128]], channel_multiplier=1).then_inc(consts, 1)
            g.memset(ones_1, 1.0).then_inc(ones_ready, 1)
            pool.wait_ge(par_in, 16 * 9)
            g.tensor_copy(par_rows[0:ST, :].rearrange("t (g p) -> t g p", g=2),
                          log_steps.unsqueeze(2).to_broadcast([ST, 2, P])).then_inc(ls_rows, 1)
            g.memset(vT[:, :, 0:W - 1], 0.0).then_inc(consts, 1)
            link(g.memset(gmask, 1.0))
            link(g.affine_select(out=gmask, in_=gmask, compare_op=ALU.is_ge, fill=0.0, base=0,
                                 pattern=[[-H, 8]], channel_multiplier=1))
            link(g.affine_select(out=gmask, in_=gmask, compare_op=ALU.is_ge, fill=0.0, base=H - 1,
                                 pattern=[[H, 8]], channel_multiplier=-1))
            link(g.tensor_tensor(gpairs, gmask[:, 0:4], gmask[:, 4:8], ALU.add))
            link(g.tensor_tensor(pmask[:, 0, :], gpairs[:, 0:2], gpairs[:, 2:4], ALU.add))
            link(g.tensor_scalar(pmask[:, 1, :], pmask[:, 0, :], -1.0, None, ALU.mult))
            link(g.memset(hmask, 1.0))
            link(g.affine_select(out=hmask[:, 0:1], in_=hmask[:, 0:1], compare_op=ALU.is_ge, fill=0.0, base=P - 1,
                                 pattern=[[0, 1]], channel_multiplier=-1))
            link(g.affine_select(out=hmask[:, 1:2], in_=hmask[:, 1:2], compare_op=ALU.is_ge, fill=0.0, base=-P,
                                 pattern=[[0, 1]], channel_multiplier=1))
            pool.wait_ge(c_in, 32)
            for ri in range(2):
                for ct in range(2):
                    ins = g.tensor_tensor(grid(at(23, 128, (2 * ct + ri) * 128), 2, P),
                                          cld[:, ri, ct, :].unsqueeze(1).to_broadcast([128, 2, P]),
                                          pmask[:, ri, :].unsqueeze(2).to_broadcast([128, 2, P]), ALU.mult)
            ins.then_inc(raw_ready, 1)
            link(g.memset(esel[:, :], 0.0))
            for s in range(3):
                link(g.affine_select(out=esel[:, :], in_=esel[:, :], compare_op=ALU.not_equal, fill=1.0,
                                     base=-E * s, pattern=[[-1, E + 1]], channel_multiplier=1))
            g.memset(esel[:, E:E + 1], 0.0).then_inc(consts, 1)
            g.iota(iota[:, :], pattern=[[1, T]], base=0, channel_multiplier=0,
                   allow_small_or_imprecise_dtypes=True).then_inc(consts, 1)
            pool.wait_ge(dve_f, 1)
            for ri in range(2):
                for ct in range(2):
                    ins = g.tensor_tensor(grid(at(11, 128, (2 * ct + ri) * 128), 4, 2, H),
                                          bbar[:, ri, 4 * ct:4 * ct + 4, :].unsqueeze(2).to_broadcast([128, 4, 2, H]),
                                          hmask.unsqueeze(1).unsqueeze(3).to_broadcast([128, 4, 2, H]), ALU.mult)
            ins.then_inc(raw_ready, 1)
            pool.wait_ge(act_sin, 2)
            link(g.memset(cosT[:, :, 0:1], 1.0))
            link(g.memset(sinT[:, :, 0:1], 0.0))
            for k in range(LEVELS):
                L = 1 << k
                pc = pw[:, k, 0, :].unsqueeze(2).to_broadcast([128, ST, L])
                ps = pw[:, k, 1, :].unsqueeze(2).to_broadcast([128, ST, L])
                lo, hi = slice(0, L), slice(L, 2 * L)
                ta, tb = (grid(t[:, 0:ST * L], ST, L) for t in tab_tmp)
                g.tensor_tensor(cosT[:, :, hi], cosT[:, :, lo], pc, ALU.mult)
                g.tensor_tensor(ta, sinT[:, :, lo], ps, ALU.mult)
                g.tensor_tensor(sinT[:, :, hi], cosT[:, :, lo], ps, ALU.mult)
                link(g.tensor_tensor(tb, sinT[:, :, lo], pc, ALU.mult))
                g.tensor_tensor(cosT[:, :, hi], cosT[:, :, hi], ta, ALU.subtract)
                last = g.tensor_tensor(sinT[:, :, hi], sinT[:, :, hi], tb, ALU.add)
                if k == LEVELS - 1:
                    last.then_inc(tables, 1)
                else:
                    link(last)
                    c0, s0, c1, s1 = pw[:, k, 0, :], pw[:, k, 1, :], pw[:, k + 1, 0, :], pw[:, k + 1, 1, :]
                    g.tensor_tensor(c1, c0, c0, ALU.mult)
                    g.tensor_tensor(pool_tmp, s0, s0, ALU.mult)
                    link(g.tensor_tensor(s1, c0, s0, ALU.mult))
                    g.tensor_tensor(c1, c1, pool_tmp, ALU.subtract)
                    link(g.tensor_tensor(s1, s1, s1, ALU.add))
            pool.wait_ge(tables, 1)
            for t in range(ST):
                pool.wait_ge(bu_sb, t + 1)
                if t >= 2:
                    pool.wait_ge(scanned, t - 1)
                b_, w_ = bu[t % 2], wz[t % 2]
                cb = cosT[:, t, :].unsqueeze(1).to_broadcast([128, 2, T])
                sb_ = sinT[:, t, :].unsqueeze(1).to_broadcast([128, 2, T])
                g.tensor_tensor(w_, b_, cb, ALU.mult)
                link(g.tensor_tensor(q_pool, b_, sb_, ALU.mult))
                g.tensor_tensor(w_[:, 0, :], w_[:, 0, :], q_pool[:, 1, :], ALU.add)
                last = g.tensor_tensor(w_[:, 1, :], w_[:, 1, :], q_pool[:, 0, :], ALU.subtract)
                last.then_inc(turned, 1)
                pool.wait_ge(turned, t + 1)
            g.memset(rank[:, :, E:E + 1], -1.0).then_inc(consts, 1)
            g.memset(gate[:, :, E:E + 1], 0.0).then_inc(consts, 1)
            g.memset(spT[:, :, :, :], 0.0).then_inc(spT_sb, 1)
            pool.wait_ge(y_pe, ST)
            g.memset(ones, 1.0).then_inc(consts, 1)
            link(g.memset(tri, 1.0))
            g.affine_select(out=tri, in_=tri, compare_op=ALU.is_gt, fill=0.0, base=0,
                            pattern=[[1, 128]], channel_multiplier=-1).then_inc(consts, 1)

        @block.scalar
        def _(act):
            s = nc.scalar
            for t in range(TT):
                act.wait_ge(x_in[t], 16)
                s.activation(squares[:, t, :], x_sb[:, t, :], ACT.Square, accum_out=ss[:, t:t + 1]).then_inc(x_sq, 1)
            act.wait_ge(var_x, 1)
            s.activation(rstd, ss, ACT.Sqrt).then_inc(std_x, 1)
            act.wait_ge(params_pe, 1)
            s.activation(par[:, :], bank[7][:, 0:54], ACT.Copy).then_inc(params_sb, 1)
            act.wait_ge(spread_pe, 1)
            s.activation(rstd_all, bank[6][:, 0:T], ACT.Copy).then_inc(rstd_sb, 1)
            act.wait_ge(params_sb, 1)
            s.activation(dt8, p_ls, ACT.Exp).then_inc(act_dt, 1)
            act.wait_ge(params_pe, 2)
            s.activation(taps[:, :, :], bank[7][:, 64:64 + KC * W].rearrange("p (k w) -> p k w", w=W), ACT.Copy)\
                .then_inc(params_sb, 1)
            act.wait_ge(dve_th, 1)
            s.activation(mag, lrdt, ACT.Exp).then_inc(act_mag, 1)
            act.wait_ge(dve_rr, 1)
            s.activation(pw[:, 0, 1, :], rr, ACT.Sin).then_inc(act_sin, 1)
            s.activation(pw[:, 0, 0, :], ra, ACT.Sin).then_inc(act_sin, 1)

            def take(n):
                c = ORDER[n]
                src = bank[4 + n % 4][:, :]
                act.wait_ge(win_pe, n + 1)
                if c in (3, 4, 5):
                    if c > 3:
                        act.wait_ge(win_dve, c - 3)
                    s.activation(sig_a, grid(src, 2, T), ACT.Sigmoid).then_inc(win_act, 1)
                elif c == 6:
                    s.activation(uT, grid(src, 2, T), ACT.Copy).then_inc(win_act, 1)
                elif c < 11:
                    s.activation(gateC[:, 2 * (c - 7):2 * (c - 7) + 2, :], grid(src, 2, T), ACT.Sigmoid).then_inc(win_act, 1)
                else:
                    s.activation(gateS[:, 2 * (c - 11):2 * (c - 11) + 2, :], grid(src, 2, T), ACT.Sigmoid).then_inc(win_act, 1)

            def bu_copy(t):
                act.wait_ge(bu_pe, t + 1)
                if t >= 2:
                    act.wait_ge(turned, t - 1)
                s.activation(bu[t % 2], grid(bank[t % 2][:, :], 2, T), ACT.Copy).then_inc(bu_sb, 1)

            take(0)
            act.wait_ge(rawT_pe, 1)
            s.activation(cT, grid(bank[0][:, :], 2, 2, 128), ACT.Copy).then_inc(rawT_sb, 1)
            take(2)
            act.wait_ge(rawT_pe, 2)
            s.activation(bT, grid(bank[1][:, :], 2, 2, 128), ACT.Copy).then_inc(rawT_sb, 1)
            take(4)
            take(5)
            bu_copy(0)
            bu_copy(1)
            bu_copy(2)
            take(7)
            bu_copy(3)
            act.wait_ge(tables, 1)
            for n in (8, 9, 10, 11):
                take(n)
                bu_copy(n - 4)
            for n in (12, 13):
                take(n)
            act.wait_ge(y_pre, 1)
            s.activation(ygelu, yglu, ACT.Gelu_apprx_tanh).then_inc(y_gelu, 1)
            for k in range(KC):
                act.wait_ge(centred, k + 1)
                s.activation(silu[:, k, :], conv[:, k, :], ACT.Square).then_inc(conv_sq, 1)
            take(14)
            act.wait_ge(glu_pe, 1)
            for m in range(2):
                s.activation(uT[:, m, :], bank[2][:, m * T:m * T + T], ACT.Sigmoid, bias=p_bg[:, m:m + 1]).then_inc(glu_sig, 1)
            act.wait_ge(var_c, 1)
            s.activation(rstdc, rstdc, ACT.Sqrt).then_inc(std_c, 1)
            for k in range(KC):
                act.wait_ge(scaled, k + 1)
                s.activation(silu[:, k, :], conv[:, k, :], ACT.Silu, scale=p_lg[:, k:k + 1], bias=p_lb[:, k:k + 1])\
                    .then_inc(silu_ready, 1)
            for t in range(TT):
                if t == 0:
                    act.wait_ge(x1_pe, 1)
                else:
                    act.wait_ge(wout_used, 4)
                for h in range(2):
                    last = s.activation(area[:, 512 * h + 1024 * t:512 * h + 1024 * t + 512], bank[2 * t + h][:, :], ACT.Square,
                                        accum_out=ss4[:, 2 * t + h:2 * t + h + 1])
                last.then_inc(x1_sq, 1)
                act.wait_ge(var_h, t + 1)
                s.activation(rstd[:, t:t + 1], ss[:, t:t + 1], ACT.Sqrt).then_inc(std_h, 1)
                act.wait_ge(h2T_pe, 2 * t + 1)
                s.activation(h2T[:, t, 0:4, :], grid(bank[4 + 2 * t][:, :], 4, 128), ACT.Copy).then_inc(h2T_act, 1)
            for t in range(TT):
                act.wait_ge(top8, t + 1)
                s.activation(pe4[:, t, :], v8[:, t, 0:TOPK], ACT.Exp, bias=neg_top[:, t:t + 1],
                             accum_out=top_sum[:, t:t + 1]).then_inc(probs, 1)
            act.wait_ge(gmT_pe, 1)
            s.activation(gmT, bank[7][0:E, 0:T], ACT.Copy).then_inc(gmT_sb, 1)

            def h_row_copy():
                return s.activation(hrow, bank[6][:, :], ACT.Copy)

            def h_T_copy():
                return s.activation(heT, grid(bank[7][:, :], 4, 128), ACT.Copy)

            def a_T_copy():
                return s.activation(actT, grid(bank[4][:, :], 4, 128), ACT.Copy)

            def y_row_copy():
                return s.activation(yrow, bank[6][:, :], ACT.Copy)

            def sigmoid():
                return s.activation(sg, gc, ACT.Sigmoid, scale=1.702)

            def spread_copy():
                s.activation(spT[0:64, 0, :, :], grid(bank[5][0:64, 0:T], 2, 128), ACT.Copy)
                return s.activation(spT[64:128, 1, :, :], grid(bank[5][64:128, 0:T], 2, 128), ACT.Copy)

            act.wait_ge(h_pe, 1)
            h_row_copy().then_inc(h_row, 1)
            act.wait_ge(hT_pe, 1)
            h_T_copy().then_inc(h_T, 1)
            act.wait_ge(nums_ready, 1)
            any_more = act.value_load(nums[0:1, 2 * E:2 * E + 1], min_val=0, max_val=E)
            with act.Fori(0, E // 2) as i:
                for half in range(2):
                    e = i * 2 + half
                    act.wait_ge(g_clip, e + 1)
                    sigmoid().then_inc(g_sig, 1)
                    act.wait_ge(h_pe, e + 2)
                    h_row_copy().then_inc(h_row, 1)
                    act.wait_ge(aT_pe, e + 1)
                    a_T_copy().then_inc(a_T, 1)
                    act.wait_ge(hT_pe, e + 2)
                    h_T_copy().then_inc(h_T, 1)
                    act.wait_ge(spT_pe, e + 1)
                    spread_copy().then_inc(spT_sb, 1)
                    act.wait_ge(chunk_used, e * PER + PER)
                    y_row_copy().then_inc(y_row, 1)
                    with act.If(any_more > 0):
                        over = act.value_load(nums[0:1, bass.ds(e, 1)], min_val=0, max_val=1)
                        with act.If(over > 0):
                            before = act.value_load(nums[0:1, bass.ds(e + E, 1)], min_val=0, max_val=E)
                            with act.Fori(0, MORE) as b:
                                o = before * MORE_STEPS + b * BLOCK_STEPS + 1
                                act.wait_ge(step, o + 3)
                                h_row_copy().then_inc(step, 1)
                                act.wait_ge(step, o + 5)
                                h_T_copy()
                                spread_copy().then_inc(step, 1)
                                act.wait_ge(step, o + 8)
                                sigmoid().then_inc(step, 1)
                                act.wait_ge(step, o + 12)
                                a_T_copy().then_inc(step, 1)
                                act.wait_ge(step, o + 14)
                                y_row_copy().then_inc(step, 1)
                            a = before * MORE_STEPS + MORE * BLOCK_STEPS + 1
                            act.wait_ge(step, a + 3)
                            h_row_copy().then_inc(step, 1)
                            act.wait_ge(step, a + 5)
                            h_T_copy().then_inc(step, 1)
                            act.wait_ge(step, a + 6)
                            act.sem_inc(passed, 1)
            s.activation(neg_top, ident[:, 0:2], ACT.Sqrt)
            for t in range(TT):
                act.wait_ge(x2_pe, t + 1)
                for h in range(2):
                    last = s.activation(at(4, 512, 512 * (2 * t + h)), bank[2 * t + h][:, :], ACT.Square,
                                        accum_out=ss4[:, 2 * t + h:2 * t + h + 1])
                last.then_inc(x2_sq, 1)
                act.wait_ge(var_f, t + 1)
                s.activation(rstd[:, t:t + 1], ss[:, t:t + 1], ACT.Sqrt).then_inc(std_f, 1)

        @block.vector
        def _(dve):
            v = nc.vector
            own = [0]

            def link(ins):
                own[0] += 1
                ins.then_inc(dve_own, 1)
                dve.wait_ge(dve_own, own[0])

            def var_of_sum(n):
                return v.tensor_scalar(ss, ss, 1.0 / n, EPS, ALU.mult, ALU.add)

            dve.wait_ge(x_sq, TT)
            var_of_sum(D).then_inc(var_x, 1)
            dve.wait_ge(std_x, 1)
            link(v.reciprocal(rstd, rstd))
            dve.wait_ge(consts, 1)
            for t in range(TT):
                v.tensor_scalar(diag[:, t, :], ident[:, :], rstd[:, t:t + 1], None, ALU.mult).then_inc(diag_ready, 1)
            dve.wait_ge(params_sb, 1)
            dve.wait_ge(rstd_sb, 1)
            for k in range(KD):
                v.scalar_tensor_tensor(hT[:, k, :], bank[k // 2][:, k % 2 * T:k % 2 * T + T], p_g[:, k:k + 1],
                                       rstd_all, ALU.mult, ALU.mult).then_inc(hT_ready, 1)
            dve.wait_ge(act_dt, 1)
            v.tensor_tensor(th, p_im, dt8, ALU.mult)
            link(v.tensor_tensor(lrdt, p_re, dt8, ALU.mult))
            link(v.tensor_scalar(kk, th, 1.0 / TWO_PI, ROUND, ALU.mult, ALU.add))
            v.tensor_scalar(kk, kk, -ROUND, None, ALU.add).then_inc(dve_th, 1)
            dve.wait_ge(dve_th, 1)
            link(v.scalar_tensor_tensor(rr, kk, -C1, th, ALU.mult, ALU.add))
            link(v.scalar_tensor_tensor(rr, kk, -C2, rr, ALU.mult, ALU.add))
            link(v.scalar_tensor_tensor(rr, kk, -C3, rr, ALU.mult, ALU.add))
            link(v.tensor_scalar(rr, rr, 3.1415925, -3.1415925, ALU.min, ALU.max))
            link(v.scalar_tensor_tensor(ra, rr, -1.0, rr, ALU.mult, ALU.max))
            v.tensor_scalar(ra, ra, -1.0, TWO_PI / 4, ALU.mult, ALU.add).then_inc(dve_rr, 1)
            v.tensor_tensor(t1, p_re, p_re, ALU.mult)
            link(v.tensor_tensor(t2, p_im, p_im, ALU.mult))
            link(v.tensor_tensor(den, t1, t2, ALU.add))
            link(v.reciprocal(den, den))
            dve.wait_ge(act_mag, 1)
            dve.wait_ge(act_sin, 2)
            v.tensor_tensor(t1, mag, pw[:, 0, 0, :], ALU.mult)
            link(v.tensor_tensor(t2, mag, pw[:, 0, 1, :], ALU.mult))
            link(v.tensor_scalar(t1, t1, -1.0, None, ALU.add))
            v.tensor_tensor(fr, t1, p_re, ALU.mult)
            v.tensor_tensor(kk, t2, p_im, ALU.mult)
            v.tensor_tensor(fi, t2, p_re, ALU.mult)
            link(v.tensor_tensor(th, t1, p_im, ALU.mult))
            v.tensor_tensor(fr, fr, kk, ALU.add)
            link(v.tensor_tensor(fi, fi, th, ALU.subtract))
            v.tensor_tensor(fr, fr, den, ALU.mult)
            link(v.tensor_tensor(fi, fi, den, ALU.mult))
            dve.wait_ge(ssm_in, 32)
            frb = fr.unsqueeze(2).to_broadcast([128, ST, H])
            fib = fi.unsqueeze(2).to_broadcast([128, ST, H])
            link(v.tensor_tensor(btmp[:, :, :], ssb[:, 1, :, :], fib, ALU.mult))
            link(v.tensor_tensor(bbar[:, 0, :, :], ssb[:, 0, :, :], frb, ALU.mult))
            link(v.tensor_tensor(bbar[:, 0, :, :], bbar[:, 0, :, :], btmp[:, :, :], ALU.subtract))
            link(v.tensor_tensor(btmp[:, :, :], ssb[:, 0, :, :], fib, ALU.mult))
            link(v.tensor_tensor(bbar[:, 1, :, :], ssb[:, 1, :, :], frb, ALU.mult))
            v.tensor_tensor(bbar[:, 1, :, :], bbar[:, 1, :, :], btmp[:, :, :], ALU.add).then_inc(dve_f, 1)
            def gated(j):
                n = ORDER.index(j)
                dve.wait_ge(win_pe, n + 1)
                dve.wait_ge(win_act, (1, 2, 4)[j])
                v.tensor_tensor(vT[:, 2 * j:2 * j + 2, W - 1:PADT], sig_a, grid(bank[4 + n % 4][:, :], 2, T),
                                ALU.mult).then_inc(win_dve, 1)
                dve.wait_ge(win_dve, j + 1)

            last_tap = {}

            def taps_of(j, ws):
                for w in ws:
                    for k in (2 * j, 2 * j + 1):
                        src = vT[:, k, w:w + T]
                        if w == 0:
                            ins = v.tensor_scalar(conv[:, k, :], src, taps[:, k, 0:1], p_cb[:, k:k + 1], ALU.mult, ALU.add)
                        else:
                            dve.wait_ge(dve_own, last_tap[k])
                            ins = v.scalar_tensor_tensor(conv[:, k, :], src, taps[:, k, w:w + 1], conv[:, k, :],
                                                         ALU.mult, ALU.add)
                        if w == W - 1:
                            ins.then_inc(conv_done, 1)
                        else:
                            own[0] += 1
                            last_tap[k] = own[0]
                            ins.then_inc(dve_own, 1)

            dve.wait_ge(consts, 2)
            gated(0)
            dve.wait_ge(raw_ready, 1)
            dve.wait_ge(params_sb, 2)
            taps_of(0, range(W))
            gated(1)
            taps_of(1, range(W))
            gated(2)
            for t in range(ST):
                dve.wait_ge(turned, t + 1)
                if t == 0:
                    dve.wait_ge(rawT_pe, 1)
                for ri in range(2):
                    last = v.tensor_tensor_scan(zz[:, ri, :], mag[:, t:t + 1].to_broadcast([128, T]), wz[t % 2][:, ri, :],
                                                0.0, ALU.mult, ALU.add)
                last.then_inc(scanned, 1)
                dve.wait_ge(scanned, t + 1)
                if t >= NX:
                    dve.wait_ge(y_pe, t - NX + 1)
                cb = cosT[:, t, :].unsqueeze(1).to_broadcast([128, 2, T])
                sb_ = sinT[:, t, :].unsqueeze(1).to_broadcast([128, 2, T])
                v.tensor_tensor(xs[t % NX], zz, cb, ALU.mult)
                link(v.tensor_tensor(q_dve, zz, sb_, ALU.mult))
                v.tensor_tensor(xs[t % NX][:, 0, :], xs[t % NX][:, 0, :], q_dve[:, 1, :], ALU.subtract)
                v.tensor_tensor(xs[t % NX][:, 1, :], xs[t % NX][:, 1, :], q_dve[:, 0, :], ALU.add).then_inc(states, 1)
                taps_of(2, range(SCAN_TAPS * t, SCAN_TAPS * (t + 1) if t < ST - 1 else W))
                dve.wait_ge(states, t + 1)
            dve.wait_ge(conv_done, KC)
            dve.wait_ge(y_pe, ST)
            dve.wait_ge(turned, ST)
            for c in range(2):
                last = v.scalar_tensor_tensor(yglu[:, c, :], uT[:, c, :], p_d[:, c:c + 1], bank[3][:, c * T:c * T + T],
                                              ALU.mult, ALU.add)
            last.then_inc(y_pre, 1)
            dve.wait_ge(mean_pe, 1)
            link(v.tensor_scalar(mean, bank[0][:, 0:T], 1.0 / DC, None, ALU.mult))
            for k in range(KC):
                v.tensor_tensor(conv[:, k, :], conv[:, k, :], mean, ALU.subtract).then_inc(centred, 1)
            dve.wait_ge(glu_sig, 2)
            v.tensor_tensor(yglu, ygelu, uT, ALU.mult).then_inc(y_glu, 1)
            dve.wait_ge(var_pe, 1)
            v.tensor_scalar(rstdc, bank[1][:, 0:T], 1.0 / DC, EPS, ALU.mult, ALU.add).then_inc(var_c, 1)
            dve.wait_ge(std_c, 1)
            link(v.reciprocal(rstdc, rstdc))
            dve.wait_ge(centred, KC)
            for k in range(KC):
                v.tensor_tensor(conv[:, k, :], conv[:, k, :], rstdc, ALU.mult).then_inc(scaled, 1)
            dve.wait_ge(bias_in, 48)
            for n in (96, 64):
                link(v.tensor_copy(biasb[0:n, :], bias32[0:n, :]))
                link(v.tensor_tensor(bias32[0:n, :], bias32[0:n, :], biasb[0:n, :], ALU.subtract))
            v.tensor_copy(biasb[0:32, :], bias32[0:32, :]).then_inc(biasb_ready, 1)
            dve.wait_ge(win_act, 12)
            for j in range(4):
                dve.wait_ge(ssm_pe, j + 1)
                v.tensor_tensor(gateS[:, 2 * j:2 * j + 2, :], gateS[:, 2 * j:2 * j + 2, :],
                                grid(bank[(2, 3, 0, 1)[j]][:, :], 2, T), ALU.mult).then_inc(ssm_gated, 1)
            dve.wait_ge(ssm_gated, 4)
            for j in range(4):
                dve.wait_ge(conv_pe, j + 1)
                link(v.tensor_tensor(gateC[:, 2 * j:2 * j + 2, :], gateC[:, 2 * j:2 * j + 2, :],
                                     grid(bank[4 + j][:, :], 2, T), ALU.mult))
                v.tensor_tensor(gateC[:, 2 * j:2 * j + 2, :], gateC[:, 2 * j:2 * j + 2, :], gateS[:, 2 * j:2 * j + 2, :],
                                ALU.add).then_inc(mixed, 1)

            def row_var(t):
                link(v.tensor_tensor(ss[:, t:t + 1], ss4[:, 2 * t:2 * t + 1], ss4[:, 2 * t + 1:2 * t + 2], ALU.add))
                return v.tensor_scalar(ss[:, t:t + 1], ss[:, t:t + 1], 1.0 / D, EPS, ALU.mult, ALU.add)

            def normed(t, dst, g, ready):
                link(v.reciprocal(rstd[:, t:t + 1], rstd[:, t:t + 1]))
                for h in range(2):
                    c = slice(h * 512, h * 512 + 512)
                    last = v.scalar_tensor_tensor(dst[:, c], bank[2 * t + h][:, :], rstd[:, t:t + 1], g[:, c], ALU.mult, ALU.mult)
                    last.then_inc(ready, 1)

            dve.wait_ge(ffn_in, 48)
            dve.wait_ge(consts, 4)
            selv = sel.rearrange("p (t k) e -> p t k e", t=TT)
            for t in range(TT):
                dve.wait_ge(x1_sq, t + 1)
                row_var(t).then_inc(var_h, 1)
                dve.wait_ge(std_h, t + 1)
                normed(t, rows[:, t, :], gffn, h_ready)
                dve.wait_ge(h2T_pe, 2 * t + 2)
                v.tensor_copy(h2T[:, t, 4:8, :], grid(bank[5 + 2 * t][:, :], 4, 128)).then_inc(h2T_dve, 1)
                dve.wait_ge(logits_pe, t + 1)
                link(v.tensor_copy(lg[:, t, :], bank[4 + 2 * t][:, 0:E]))
                link(v.max(out=v8[:, t, :], in_=lg[:, t, :]))
                v.tensor_scalar(neg_top[:, t:t + 1], v8[:, t, 0:1], -1.0, None, ALU.mult).then_inc(top8, 1)
                link(v.max_index(out=idx8[:, t, :], in_max=v8[:, t, :], in_values=lg[:, t, :]))
                link(v.tensor_copy(idxf[:, t, :], idx8[:, t, :]))
                link(v.tensor_tensor(selv[:, t], iota[:, 0:E].unsqueeze(1).to_broadcast([128, TOPK, E]),
                                     idxf[:, t, 0:TOPK].unsqueeze(2).to_broadcast([128, TOPK, E]), ALU.is_equal))
                v.tensor_reduce(mask[:, t, :], selv[:, t].rearrange("p k e -> p e k"), AX.X, ALU.add).then_inc(mask_ready, 1)
            dve.wait_ge(probs, TT)
            link(v.reciprocal(top_sum, top_sum))
            for t in range(TT):
                last = v.tensor_scalar(pe4[:, t, :], pe4[:, t, :], top_sum[:, t:t + 1], None, ALU.mult)
            link(last)
            dve.wait_ge(mask_ready, TT)
            for t in range(TT):
                last = v.tensor_tensor(selv[:, t], selv[:, t], pe4[:, t, :].unsqueeze(2).to_broadcast([128, TOPK, E]), ALU.mult)
            link(last)
            for t in range(TT):
                last = v.tensor_reduce(gate[:, t, 0:E], selv[:, t].rearrange("p k e -> p e k"), AX.X, ALU.add)
            last.then_inc(gates_ready, 1)
            dve.wait_ge(cum_pe, 1)
            link(v.scalar_tensor_tensor(rank[:, :, 0:E], grid(bank[5][:, 0:TT * E], TT, E), 1.0, mask, ALU.add, ALU.mult))
            link(v.tensor_scalar(rank[:, :, 0:E], rank[:, :, 0:E], -1.0, None, ALU.add))
            def picks(e, slot, buf):
                for t in range(TT):
                    v.tensor_scalar(pick[:, t, :], slot, rank[:, t, bass.ds(e, 1)], None, ALU.is_equal)
                return v.tensor_copy(onehot[:, buf, :], esel[:, bass.ds(e, 1)].to_broadcast([96, CAP]))

            def spreads(e, slot):
                both = slot.unsqueeze(1).to_broadcast([128, 2, CAP])
                for t in range(TT):
                    last = v.tensor_scalar(spread[:, t, :, :], both, rank[:, t, bass.ds(e, 1)], gate[:, t, bass.ds(e, 1)],
                                           ALU.is_equal, ALU.mult)
                return last

            def clip_gate():
                return v.tensor_scalar(gc, bank[4][:, :], 7.0, None, ALU.min)

            def clip_lin():
                return v.tensor_scalar(lc, bank[5][:, :], 7.0, -7.0, ALU.min, ALU.max)

            def lin_times_gate():
                return v.scalar_tensor_tensor(lc, lc, 1.0, gc, ALU.add, ALU.mult)

            def times_sigmoid():
                return v.tensor_tensor(lc, lc, sg, ALU.mult)

            first = iota[:, 0:CAP]
            picks(0, first, 0).then_inc(pick_ready, 1)
            over_f, upto, before_f = numf[:, 0:E], numf[:, E + 1:2 * E + 1], numf[:, 2 * E + 1:3 * E + 1]
            link(v.tensor_scalar(over_f, bank[5][0:1, 2 * E:3 * E], float(CAP), None, ALU.is_gt))
            link(v.tensor_tensor_scan(upto, over_f, over_f, 0.0, ALU.add, ALU.bypass))
            link(v.tensor_tensor(before_f, upto, over_f, ALU.subtract))
            v.tensor_copy(nums[:, 0:E], over_f).then_inc(step, 1)
            v.tensor_copy(nums[:, E:2 * E], before_f)
            v.tensor_copy(nums[:, 2 * E:2 * E + 1], upto[:, E - 1:E]).then_inc(nums_ready, 1)
            dve.wait_ge(nums_ready, 1)
            v.memset(yrow, 0.0).then_inc(y_row, 1)
            any_more = dve.value_load(nums[0:1, 2 * E:2 * E + 1], min_val=0, max_val=E)
            with dve.Fori(0, E // 2) as i:
                for half in range(2):
                    e = i * 2 + half
                    dve.wait_ge(h_pe, e + 1)
                    picks(e + 1, first, 1 - half).then_inc(pick_ready, 1)
                    dve.wait_ge(chunk_used, e * PER + KD)
                    clip_gate().then_inc(g_clip, 1)
                    clip_lin().then_inc(lin_ready, 1)
                    spreads(e, first).then_inc(spread_ready, 1)
                    dve.wait_ge(lin_ready, e + 1)
                    lin_times_gate().then_inc(swi, 1)
                    dve.wait_ge(swi, e + 1)
                    dve.wait_ge(g_sig, e + 1)
                    times_sigmoid().then_inc(act_ready, 1)
                    with dve.If(any_more > 0):
                        over = dve.value_load(nums[0:1, bass.ds(e, 1)], min_val=0, max_val=1)
                        with dve.If(over > 0):
                            before = dve.value_load(nums[0:1, bass.ds(e + E, 1)], min_val=0, max_val=E)
                            with dve.Fori(0, MORE) as b:
                                o = before * MORE_STEPS + b * BLOCK_STEPS + 1
                                slot = iota[:, bass.ds(b * CAP + CAP, CAP)]
                                dve.wait_ge(step, o + 1)
                                picks(e, slot, half)
                                spreads(e, slot).then_inc(step, 1)
                                dve.wait_ge(step, o + 7)
                                clip_lin()
                                clip_gate().then_inc(step, 1)
                                dve.wait_ge(step, o + 9)
                                lin_times_gate().then_inc(step, 1)
                                dve.wait_ge(step, o + 10)
                                times_sigmoid().then_inc(step, 1)
                            a = before * MORE_STEPS + MORE * BLOCK_STEPS + 1
                            dve.wait_ge(step, a + 1)
                            v.memset(yrow, 0.0)
                            picks(e + 1, first, 1 - half).then_inc(step, 1)
                            dve.wait_ge(step, a + 6)
                            dve.sem_inc(passed, 1)
            dve.wait_ge(fin_in, 16)
            for t in range(TT):
                dve.wait_ge(x2_sq, t + 1)
                row_var(t).then_inc(var_f, 1)
                dve.wait_ge(std_f, t + 1)
                normed(t, at(1 + t, D), at(0, D), o_ready)

        @block.tensor
        def _(pe):
            mm, tr = nc.tensor.matmul, nc.tensor.transpose
            pe.wait_ge(consts, 1)
            for t in range(TT):
                pe.wait_ge(x_in[t], 16)
                for k in range(KD):
                    tr(bank[k // 2][:, (k % 2) * T + t * 128:(k % 2) * T + t * 128 + 128],
                       x_sb[:, t, k * 128:k * 128 + 128], ident[:, :])
            pe.wait_ge(par_in, 16 * 9)
            pe.wait_ge(ls_rows, 1)
            tr(bank[7][:, 0:54], par_rows[:, :], ident[0:54, 0:54]).then_inc(params_pe, 1)
            pe.wait_ge(ones_ready, 1)
            for t in range(TT):
                pe.wait_ge(diag_ready, t + 1)
                last = mm(bank[6][:, t * 128:t * 128 + 128], ones_1, diag[:, t, :], start=True, stop=True)
            last.then_inc(spread_pe, 1)

            ACT_TAKES = {n: i + 1 for i, n in enumerate([0, 2, 4, 5] + list(range(7, NCH)))}
            DVE_TAKES = {1: 1, 3: 2, 6: 3}

            def freed(n):
                if n in DVE_TAKES:
                    pe.wait_ge(win_dve, DVE_TAKES[n])
                else:
                    pe.wait_ge(win_act, ACT_TAKES[n])

            def project(n, ms=(0, 1)):
                if n >= 4 and 0 in ms:
                    freed(n - 4)
                pe.wait_ge(win_in[n % WRING], 16 * (n // WRING + 1))
                w = grid(at(n % WRING, CH), KD, 256)
                for m in ms:
                    for k in range(KD):
                        if n == 0 and m == 0:
                            pe.wait_ge(hT_ready, k + 1)
                        last = mm(bank[4 + n % 4][:, m * T:m * T + T], w[:, k, m * 128:m * 128 + 128], hT[:, k, :],
                                  start=(k == 0), stop=(k == KD - 1))
                if 1 in ms:
                    last.then_inc(win_pe, 1)

            def raw_transpose(raw, b):
                for ct in range(2):
                    for ri in range(2):
                        last = tr(bank[b][:, (2 * ct + ri) * 128:(2 * ct + ri) * 128 + 128], raw[:, ct, ri, :], ident[:, :])
                last.then_inc(rawT_pe, 1)

            def bu_mm(t):
                if t >= 2:
                    pe.wait_ge(bu_sb, t - 1)
                r = slice(t % 4 * 32, t % 4 * 32 + 32)
                for ri in range(2):
                    last = mm(bank[t % 2][:, ri * T:ri * T + T], bT[r, t // 4, ri, :], uT[r, t // 4, :], start=True, stop=True)
                last.then_inc(bu_pe, 1)

            def y_mm(t):
                pe.wait_ge(states, t + 1)
                r = slice(t % 4 * 32, t % 4 * 32 + 32)
                for ri in range(2):
                    last = mm(bank[3][r, t // 4 * T:t // 4 * T + T], cT[:, t // 4, ri, r], xs[t % NX][:, ri, :],
                              start=(ri == 0), stop=(ri == 1))
                last.then_inc(y_pe, 1)

            project(0)
            pe.wait_ge(tap_in, 16)
            pe.wait_ge(params_sb, 1)
            for k in range(KC):
                last = tr(bank[7][:, 64 + k * W:64 + k * W + W], tap_rows[:, k * 128:k * 128 + 128], ident[0:W, 0:W])
            last.then_inc(params_pe, 1)
            project(1)
            pe.wait_ge(raw_ready, 1)
            pe.wait_ge(params_sb, 2)
            raw_transpose(craw, 0)
            project(2)
            project(3)
            pe.wait_ge(raw_ready, 2)
            raw_transpose(braw, 1)
            project(4)
            project(5)
            pe.wait_ge(rawT_sb, 2)
            freed(4)
            for t in range(4):
                bu_mm(t)
            project(6)
            project(7)
            for n, bs, ts in ((8, (4,), ()), (9, (5,), ()), (10, (6,), ()), (11, (7,), (0, 1, 2, 3)), (12, (), (4, 5)),
                              (13, (), ())):
                for t in bs:
                    bu_mm(t)
                project(n)
                for t in ts:
                    y_mm(t)
            project(14, (0,))
            y_mm(6)
            y_mm(7)
            pe.wait_ge(consts, 7)
            pe.wait_ge(conv_done, KC)
            pe.wait_ge(bu_sb, ST)
            for k in range(KC):
                last = mm(bank[0][:, 0:T], ones, conv[:, k, :], start=(k == 0), stop=(k == KC - 1))
            last.then_inc(mean_pe, 1)
            project(14, (1,))
            pe.wait_ge(y_gelu, 1)
            pe.wait_ge(glu_in, 16)
            for m in range(2):
                for k in range(2):
                    last = mm(bank[2][:, m * T:m * T + T], wglu[:, k, m * 128:m * 128 + 128], ygelu[:, k, :],
                              start=(k == 0), stop=(k == 1))
            last.then_inc(glu_pe, 1)
            for k in range(KC):
                pe.wait_ge(conv_sq, k + 1)
                last = mm(bank[1][:, 0:T], ones, silu[:, k, :], start=(k == 0), stop=(k == KC - 1))
            last.then_inc(var_pe, 1)
            pe.wait_ge(y_glu, 1)
            pe.wait_ge(wssm_in, 16)
            for j in range(4):
                b = (2, 3, 0, 1)[j]
                if b == 1:
                    pe.wait_ge(var_c, 1)
                for m in range(2):
                    c = (2 * j + m) * 128
                    for k in range(2):
                        last = mm(bank[b][:, m * T:m * T + T], wssm[:, k, c:c + 128], yglu[:, k, :],
                                  start=(k == 0), stop=(k == 1))
                last.then_inc(ssm_pe, 1)
            pe.wait_ge(wconv_in, 16)
            for j in range(4):
                freed(11 + j if j else 12)
                if j == 0:
                    freed(14)
                for m in range(2):
                    c = (2 * j + m) * 128
                    for k in range(KC):
                        if j == 0 and m == 0:
                            pe.wait_ge(silu_ready, k + 1)
                        last = mm(bank[4 + j][:, m * T:m * T + T], wconv[:, k, c:c + 128], silu[:, k, :],
                                  start=(k == 0), stop=(k == KC - 1))
                last.then_inc(conv_pe, 1)
                if j == 1:
                    pe.wait_ge(ssm_gated, 4)
                    for n in range(4):
                        mm(bank[n][:, :], ident[:, :], x_sb[:, n // 2, n % 2 * 512:n % 2 * 512 + 512], start=True, stop=False)
            def h2_transposes(t):
                for k in range(KD):
                    pe.wait_ge(h_ready, 2 * t + k // 4 + 1)
                    last = tr(bank[4 + 2 * t + k // 4][:, k % 4 * 128:k % 4 * 128 + 128],
                              rows[:, t, k * 128:k * 128 + 128], ident[:, :])
                    if k % 4 == 3:
                        last.then_inc(h2T_pe, 1)

            def logits(t):
                pe.wait_ge(h2T_act, t + 1)
                pe.wait_ge(h2T_dve, t + 1)
                for k in range(KD):
                    mm(bank[4 + 2 * t][:, 0:E], h2T[:, t, k, :], wrt[:, k, :], start=(k == 0), stop=False)
                mm(bank[4 + 2 * t][:, 0:E], ones[0:1, :], brow[:, :], start=False, stop=True).then_inc(logits_pe, 1)

            def stay_warm(n):
                for _ in range(n):
                    mm(bank[5][:, 0:128], ident[:, :], ident[:, :], start=True, stop=True)

            pe.wait_ge(wout_in, 16)
            pe.wait_ge(ffn_in, 48)
            for t in range(TT):
                for k in range(KD):
                    pe.wait_ge(mixed, k // 2 + 1)
                    for h in range(2):
                        last = mm(bank[2 * t + h][:, :], gateC[:, k, t * 128:t * 128 + 128], wout[:, k, h * 512:h * 512 + 512],
                                  start=False, stop=(k == KD - 1))
                    if t == 1 and k % 2:
                        last.then_inc(wout_used, 1)
                    if (t, k) == (1, 3):
                        h2_transposes(0)
                    if (t, k) == (1, 5):
                        logits(0)
                if t == 0:
                    last.then_inc(x1_pe, 1)
            stay_warm(WARM[0])
            h2_transposes(1)
            logits(1)
            stay_warm(WARM[1])
            pe.wait_ge(consts, 8)
            pe.wait_ge(mask_ready, TT)
            mm(bank[5][:, 0:E], tri, mask[:, 0, :], start=True, stop=True)
            mm(bank[5][:, E:2 * E], ones, mask[:, 0, :], start=True, stop=False)
            mm(bank[5][:, E:2 * E], tri, mask[:, 1, :], start=False, stop=True)
            mm(bank[5][0:1, 2 * E:3 * E], ones[:, 0:1], mask[:, 0, :], start=True, stop=False)
            mm(bank[5][0:1, 2 * E:3 * E], ones[:, 0:1], mask[:, 1, :], start=False, stop=True).then_inc(cum_pe, 1)
            pe.wait_ge(gates_ready, 1)
            for t in range(TT):
                last = tr(bank[7][0:E, t * 128:t * 128 + 128], gate[:, t, 0:E], ident[:, :])
            last.then_inc(gmT_pe, 1)

            def down_bias(n):
                return mm(bank[n][:, :], gmT[:, n // 2 * 128:n // 2 * 128 + 128], bdown[:, n % 2 * 512:n % 2 * 512 + 512],
                          start=False, stop=False, skip_group_check=True)

            def gather():
                for t in range(TT):
                    for h in range(2):
                        last = mm(bank[6][64 * h:64 * h + 64, :], pick[:, t, :], rows[:, t, h * 512:h * 512 + 512],
                                  start=(t == 0), stop=(t == TT - 1))
                return last

            def transposes(src, b):
                for m in range(4):
                    last = tr(bank[b][:, m * 128:m * 128 + 128], src[:, m * 128:m * 128 + 128], ident[:, :])
                return last

            def spread_transposes():
                for t in range(TT):
                    last = tr(bank[5][:, t * 128:t * 128 + 128], spread[:, t, :, :].rearrange("p a b -> p (a b)"), ident[:, :])
                return last

            def gate_up(half, buf, part=None, uses=None):
                ks = range(KD) if part is None else range(4 * part, 4 * part + 4)
                for b in range(2 if 0 in ks else 0):
                    for h in range(2):
                        mm(bank[4 + b][64 * h:64 * h + 64, :], onehot[:, buf, :], biasb[:, (2 * b + h) * 512:(2 * b + h + 1) * 512],
                           start=True, stop=False)
                for k in ks:
                    if uses is not None:
                        pe.wait_ge(slot_in[half * PER + k], uses)
                    w = at(half * PER + k, CH)
                    for b in range(2):
                        for h in range(2):
                            last = mm(bank[4 + b][64 * h:64 * h + 64, :], heT[:, k % 4, k // 4 * 64:k // 4 * 64 + 64],
                                      w[:, b * FF + h * 512:b * FF + h * 512 + 512], start=False, stop=(k == KD - 1))
                    if uses is not None:
                        last.then_inc(chunk_used, 1)
                return last

            def down(half, uses=None):
                for k in range(KD):
                    if uses is not None and k % 2 == 0:
                        pe.wait_ge(slot_in[half * PER + KD + k // 2], uses)
                    w = grid(at(half * PER + KD + k // 2, CH), 2, D)
                    for h in range(2):
                        last = mm(bank[6][64 * h:64 * h + 64, :], actT[:, k % 4, k // 4 * 64:k // 4 * 64 + 64],
                                  w[:, k % 2, h * 512:h * 512 + 512], start=(k == 0), stop=(k == KD - 1))
                    if uses is not None and k % 2:
                        last.then_inc(chunk_used, 1)
                return last

            def scatter():
                for n in range(4):
                    last = mm(bank[n][:, :], spT[:, n % 2, n // 2, :], yrow, start=False, stop=False, skip_group_check=True)
                return last

            pe.wait_ge(gmT_sb, 1)
            pe.wait_ge(down_in, 16)
            down_bias(0)
            down_bias(1)
            pe.wait_ge(pick_ready, 1)
            gather().then_inc(h_pe, 1)
            down_bias(2)
            pe.wait_ge(h_row, 1)
            pe.wait_ge(nums_ready, 1)
            transposes(hrow, 7).then_inc(hT_pe, 1)
            down_bias(3).then_inc(bdown_pe, 1)
            any_more = pe.value_load(nums[0:1, 2 * E:2 * E + 1], min_val=0, max_val=E)
            with pe.Fori(0, E // 2) as i:
                for half in range(2):
                    e = i * 2 + half
                    pe.wait_ge(h_T, e + 1)
                    pe.wait_ge(spT_sb, e + 1)
                    gate_up(half, half, 0, i * 16 + 16)
                    pe.wait_ge(pick_ready, e + 2)
                    pe.wait_ge(y_row, e + 1)
                    gather().then_inc(h_pe, 1)
                    gate_up(half, half, 1, i * 16 + 16)
                    scatter()
                    pe.wait_ge(act_ready, e + 1)
                    transposes(lc, 4).then_inc(aT_pe, 1)
                    pe.wait_ge(h_row, e + 2)
                    transposes(hrow, 7).then_inc(hT_pe, 1)
                    pe.wait_ge(spread_ready, e + 1)
                    spread_transposes().then_inc(spT_pe, 1)
                    pe.wait_ge(a_T, e + 1)
                    down(half, i * 16 + 16)
                    with pe.If(any_more > 0):
                        over = pe.value_load(nums[0:1, bass.ds(e, 1)], min_val=0, max_val=1)
                        with pe.If(over > 0):
                            before = pe.value_load(nums[0:1, bass.ds(e + E, 1)], min_val=0, max_val=E)
                            pe.wait_ge(y_row, e + 2)
                            pe.sem_inc(passed, 1)
                            with pe.Fori(0, MORE) as b:
                                o = before * MORE_STEPS + b * BLOCK_STEPS + 1
                                pe.wait_ge(step, o)
                                scatter().then_inc(step, 1)
                                pe.wait_ge(step, o + 2)
                                gather().then_inc(step, 1)
                                pe.wait_ge(step, o + 4)
                                transposes(hrow, 7)
                                spread_transposes().then_inc(step, 1)
                                pe.wait_ge(step, o + 6)
                                gate_up(half, half).then_inc(step, 1)
                                pe.wait_ge(step, o + 11)
                                transposes(lc, 4).then_inc(step, 1)
                                pe.wait_ge(step, o + 13)
                                down(half).then_inc(step, 1)
                            a = before * MORE_STEPS + MORE * BLOCK_STEPS + 1
                            pe.wait_ge(step, a)
                            scatter().then_inc(step, 1)
                            pe.wait_ge(step, a + 2)
                            gather().then_inc(step, 1)
                            pe.wait_ge(step, a + 4)
                            transposes(hrow, 7).then_inc(step, 1)
                            pe.wait_ge(step, a + 6)
                            pe.sem_inc(passed, 1)
            pe.wait_ge(y_row, E + 1)
            pe.wait_ge(spT_sb, E + 1)
            for t in range(TT):
                for h in range(2):
                    last = mm(bank[2 * t + h][:, :], spT[:, h, t, :], yrow, start=False, stop=True, skip_group_check=True)
                last.then_inc(x2_pe, 1)


_INS = ["x", "norm_mix_g", "w_in", "conv_w", "conv_b", "conv_ln_g", "conv_ln_b", "w_conv_out",
        "ssm_a_re", "ssm_a_im", "ssm_log_step", "ssm_b_re", "ssm_b_im", "ssm_c_re", "ssm_c_im", "ssm_d",
        "w_ssm_glu", "b_ssm_glu", "w_ssm_out", "w_out", "norm_ffn_g", "w_router", "b_router",
        "w_gate_up", "b_gate_up", "w_down", "b_down", "norm_final_g"]


def kernel(**inputs):
    import concourse.bacc as bacc
    from concourse.bass_utils import run_bass_kernel_spmd

    nc = bacc.Bacc("TRN2", target_bir_lowering=False, num_devices=1, dynamic_dma_scratch_size=64)
    arrays = {n: np.ascontiguousarray(inputs[n]) for n in _INS}
    args = [nc.dram_tensor(n, arrays[n].shape, F32, kind="ExternalInput").ap() for n in _INS]
    out = nc.dram_tensor("out", (1, T, D), F32, kind="ExternalOutput").ap()
    build(nc, *args, out)
    r = run_bass_kernel_spmd(nc, [arrays], core_ids=[0])
    return r.results[0]["out"]
```
